# Optimizing a Trainium2 kernel written in Bass

```python
import jax
import jax.numpy as jnp
from jax import lax
import numpy as np

D_MODEL = 1024
BATCH = 1
SEQ = 512
DEPTH = 1

HEAD_DIM = 64
PLE_DIM = 256
RMS_EPS = 1e-6
DIL_HEADS = 8
DIL_PATTERNS = ((128, 1), (512, 4), (2048, 16))
DIL_BLOCK = 128
NSA_HEADS = 8
NSA_KV_HEADS = 2
CMP_BLOCK = 32
CMP_STRIDE = 16
CMP_HIDDEN = 256
SLC_BLOCK = 64
SLC_TOP_N = 16
SLC_FORCE = 1e9
WIN_SIZE = 512
WIN_BLOCK = 128
NSA_Q_CHUNK = 64
N_EXPERTS = 64
TOP_K = 8
N_GROUPS = 8
TOP_GROUPS = 4
EXPERT_HIDDEN = 256
SHARED_HIDDEN = 256
ROUTED_SCALE = 2.5
MOE_BLOCK = 256
A_WIDTH = DIL_HEADS * HEAD_DIM
B_WIDTH = NSA_HEADS * HEAD_DIM
KV_WIDTH = NSA_KV_HEADS * HEAD_DIM
IN_SIZES = (A_WIDTH, A_WIDTH, A_WIDTH, B_WIDTH, KV_WIDTH, KV_WIDTH, KV_WIDTH, KV_WIDTH, KV_WIDTH, KV_WIDTH, 3 * NSA_HEADS, D_MODEL, D_MODEL)
IN_COLS = sum(IN_SIZES)

kernel_name = "hybrid_dilated_nsa_moe_block"

def rmsnorm(x, g):
    xf = x.astype(jnp.float32)
    r = lax.rsqrt(jnp.mean(xf * xf, axis=-1, keepdims=True) + RMS_EPS)
    return (xf * r).astype(x.dtype) * g

def alibi_slopes(n):
    return 2.0 ** (-8.0 * jnp.arange(1, n + 1, dtype=jnp.float32) / n)

def banded_attention(q, k, v, slopes, window, blk, dist_scale):
    n, L, H, dh = q.shape
    G = k.shape[2]
    rep = H // G
    nblk = -(-L // blk)
    Lp = nblk * blk
    nprev = -(-window // blk)
    span = (nprev + 1) * blk
    scale = dh ** -0.5
    slope = (slopes * dist_scale).reshape(G, rep)
    qp = jnp.pad(q, ((0, 0), (0, Lp - L), (0, 0), (0, 0)))
    kp = jnp.pad(k, ((0, 0), (nprev * blk, Lp - L), (0, 0), (0, 0)))
    vp = jnp.pad(v, ((0, 0), (nprev * blk, Lp - L), (0, 0), (0, 0)))
    qb = qp.reshape(n, nblk, blk, G, rep, dh).transpose(1, 0, 2, 3, 4, 5)

    def one_block(args):
        i, qi = args
        ki = lax.dynamic_slice_in_dim(kp, i * blk, span, axis=1)
        vi = lax.dynamic_slice_in_dim(vp, i * blk, span, axis=1)
        qpos = i * blk + jnp.arange(blk)
        kpos = (i - nprev) * blk + jnp.arange(span)
        dist = (qpos[:, None] - kpos[None, :]).astype(jnp.float32)
        valid = (dist >= 0) & (dist <= window) & (kpos[None, :] >= 0)
        s = jnp.einsum('nqgrd,nkgd->ngrqk', qi, ki).astype(jnp.float32) * scale - slope[:, :, None, None] * dist
        s = jnp.where(valid, s, -jnp.inf)
        lse = jax.nn.logsumexp(s, axis=-1)
        pr = jnp.exp(s - lse[..., None]).astype(vi.dtype)
        o = jnp.einsum('ngrqk,nkgd->nqgrd', pr, vi)
        return o, lse

    o, lse = lax.map(one_block, (jnp.arange(nblk), qb))
    o = o.transpose(1, 0, 2, 3, 4, 5).reshape(n, Lp, H, dh)[:, :L]
    lse = lse.transpose(1, 0, 4, 2, 3).reshape(n, Lp, H)[:, :L]
    return o, lse

def dilated_attention(q, k, v, slopes):
    B, S, H, dh = q.shape
    outs, lses = [], []
    for window, dil in DIL_PATTERNS:
        def split(t):
            return t.reshape(B, S // dil, dil, H, dh).transpose(0, 2, 1, 3, 4).reshape(B * dil, S // dil, H, dh)
        o, lse = banded_attention(split(q), split(k), split(v), slopes, window // dil, DIL_BLOCK, dil)
        outs.append(o.reshape(B, dil, S // dil, H, dh).transpose(0, 2, 1, 3, 4).reshape(B, S, H, dh))
        lses.append(lse.reshape(B, dil, S // dil, H).transpose(0, 2, 1, 3).reshape(B, S, H))
    w = jax.nn.softmax(jnp.stack(lses, axis=0), axis=0).astype(q.dtype)
    out = w[0][..., None] * outs[0]
    for g in range(1, len(DIL_PATTERNS)):
        out = out + w[g][..., None] * outs[g]
    return out

def compress_blocks(t, pos, w1, b1, w2):
    B, S, G, dh = t.shape
    nparts = CMP_BLOCK // CMP_STRIDE
    nchunk = S // CMP_STRIDE
    ncmp = nchunk - nparts + 1
    tc = t.reshape(B, nchunk, CMP_STRIDE, G, dh)
    blocks = jnp.concatenate([tc[:, j:j + ncmp] for j in range(nparts)], axis=2)
    blocks = blocks + pos[:, None, :]
    flat = blocks.transpose(0, 1, 3, 2, 4).reshape(B, ncmp, G, CMP_BLOCK * dh)
    return jax.nn.gelu(flat @ w1 + b1) @ w2

def nsa_attention(q, kc, vc, ks, vs, kw, vw, gates, slopes):
    B, S, H, dh = q.shape
    G = kc.shape[2]
    rep = H // G
    scale = dh ** -0.5
    slope = slopes.reshape(G, rep)
    ncmp = kc.shape[1]
    nslc = S // SLC_BLOCK
    n_sel = min(SLC_TOP_N, nslc)
    C = NSA_Q_CHUNK
    nq = S // C
    cmp_end = jnp.arange(ncmp) * CMP_STRIDE + (CMP_BLOCK - 1)
    ci = jnp.arange(ncmp)[:, None]
    sj = jnp.arange(nslc)[None, :]
    overlap = ((ci * CMP_STRIDE < (sj + 1) * SLC_BLOCK) & (ci * CMP_STRIDE + CMP_BLOCK > sj * SLC_BLOCK)).astype(jnp.float32)
    ks_blk = ks.reshape(B, nslc, SLC_BLOCK, G, dh).transpose(0, 3, 1, 2, 4)
    vs_blk = vs.reshape(B, nslc, SLC_BLOCK, G, dh).transpose(0, 3, 1, 2, 4)
    b_ix = jnp.arange(B)[:, None, None, None]
    g_ix = jnp.arange(G)[None, :, None, None]
    blk_ix = jnp.arange(nslc)
    in_blk = jnp.arange(SLC_BLOCK)
    qc = q.reshape(B, nq, C, G, rep, dh).transpose(1, 0, 2, 3, 4, 5)

    def chunk(args):
        c, qi = args
        tpos = c * C + jnp.arange(C)
        dist = (tpos[:, None] - cmp_end[None, :]).astype(jnp.float32)
        s = jnp.einsum('bqgrd,bkgd->bgrqk', qi, kc).astype(jnp.float32) * scale - slope[:, :, None, None] * dist
        s = jnp.where(dist >= 0, s, -jnp.inf)
        m = jnp.max(s, axis=-1, keepdims=True)
        m = jnp.where(jnp.isfinite(m), m, 0.0)
        e = jnp.exp(s - m)
        den = jnp.sum(e, axis=-1, keepdims=True)
        pc = e / jnp.where(den > 0, den, 1.0)
        o_cmp = jnp.einsum('bgrqk,bkgd->bqgrd', pc.astype(vc.dtype), vc)
        p_slc = jnp.einsum('bgrqk,kj->bgqj', pc, overlap)
        cur = tpos // SLC_BLOCK
        forced = (blk_ix[None, :] == 0) | (blk_ix[None, :] == cur[:, None]) | (blk_ix[None, :] == cur[:, None] - 1)
        future = blk_ix[None, :] * SLC_BLOCK > tpos[:, None]
        score = jnp.where(forced, SLC_FORCE, jnp.where(future, -SLC_FORCE, p_slc))
        _, idx = lax.top_k(score, n_sel)
        kg = ks_blk[b_ix, g_ix, idx]
        vg = vs_blk[b_ix, g_ix, idx]
        kpos = idx[..., None] * SLC_BLOCK + in_blk
        dist2 = (tpos[None, None, :, None, None] - kpos).astype(jnp.float32)[:, :, None]
        s2 = jnp.einsum('bqgrd,bgqnkd->bgrqnk', qi, kg).astype(jnp.float32) * scale - slope[None, :, :, None, None, None] * dist2
        s2 = jnp.where(dist2 >= 0, s2, -jnp.inf)
        p2 = jax.nn.softmax(s2.reshape(B, G, rep, C, n_sel * SLC_BLOCK), axis=-1).reshape(s2.shape)
        o_slc = jnp.einsum('bgrqnk,bgqnkd->bqgrd', p2.astype(vg.dtype), vg)
        return o_cmp, o_slc

    o_cmp, o_slc = lax.map(chunk, (jnp.arange(nq), qc))
    o_cmp = o_cmp.transpose(1, 0, 2, 3, 4, 5).reshape(B, S, H, dh)
    o_slc = o_slc.transpose(1, 0, 2, 3, 4, 5).reshape(B, S, H, dh)
    o_win, _ = banded_attention(q, kw, vw, slopes, WIN_SIZE - 1, WIN_BLOCK, 1)
    return gates[:, :, 0, :, None] * o_cmp + gates[:, :, 1, :, None] * o_slc + gates[:, :, 2, :, None] * o_win

def moe_ffn(x, w_router, router_bias, w_gate, w_up, w_down, ws_gate, ws_up, ws_down):
    B, S, D = x.shape
    N = B * S
    xf = x.reshape(N, D)
    scores = jax.nn.sigmoid((xf @ w_router).astype(jnp.float32))
    sel = scores + router_bias.astype(jnp.float32)
    gscore = jnp.sum(lax.top_k(sel.reshape(N, N_GROUPS, N_EXPERTS // N_GROUPS), 2)[0], axis=-1)
    _, gidx = lax.top_k(gscore, TOP_GROUPS)
    gmask = jnp.any(gidx[:, :, None] == jnp.arange(N_GROUPS), axis=1)
    emask = jnp.repeat(gmask, N_EXPERTS // N_GROUPS, axis=1)
    _, eidx = lax.top_k(jnp.where(emask, sel, -jnp.inf), TOP_K)
    w = jnp.take_along_axis(scores, eidx, axis=1)
    w = w / jnp.sum(w, axis=-1, keepdims=True) * ROUTED_SCALE

    NK = N * TOP_K
    nblk = (NK + N_EXPERTS * (MOE_BLOCK - 1) + MOE_BLOCK - 1) // MOE_BLOCK
    P = nblk * MOE_BLOCK
    flat_e = eidx.reshape(NK)
    flat_tok = jnp.arange(NK, dtype=jnp.int32) // TOP_K
    flat_w = w.reshape(NK)
    order = jnp.argsort(flat_e)
    se = flat_e[order]
    counts = jnp.bincount(flat_e, length=N_EXPERTS)
    padded = (counts + MOE_BLOCK - 1) // MOE_BLOCK * MOE_BLOCK
    pend = jnp.cumsum(padded)
    pstart = pend - padded
    start = jnp.cumsum(counts) - counts
    dest = pstart[se] + jnp.arange(NK) - start[se]
    row_tok = jnp.full((P,), N, dtype=jnp.int32).at[dest].set(flat_tok[order])
    row_w = jnp.zeros((P,), x.dtype).at[dest].set(flat_w[order].astype(x.dtype))
    blk_e = jnp.minimum(jnp.searchsorted(pend, jnp.arange(nblk) * MOE_BLOCK, side='right'), N_EXPERTS - 1)
    x_pad = jnp.concatenate([xf, jnp.zeros((1, D), x.dtype)], axis=0)

    def step(y, args):
        tok, wt, e = args
        xb = x_pad[tok]
        hid = jax.nn.silu(xb @ w_gate[e]) * (xb @ w_up[e])
        return y.at[tok].add((hid @ w_down[e]) * wt[:, None]), None

    y, _ = lax.scan(step, jnp.zeros((N + 1, D), x.dtype),
                    (row_tok.reshape(nblk, MOE_BLOCK), row_w.reshape(nblk, MOE_BLOCK), blk_e))
    shared = (jax.nn.silu(xf @ ws_gate) * (xf @ ws_up)) @ ws_down
    return (y[:N] + shared).reshape(B, S, D)

def setup_inputs(seed: int = 0) -> dict:
    key = jax.random.key(seed)
    ks = jax.random.split(key, 32)
    L, D, dh = DEPTH, D_MODEL, HEAD_DIM

    def nrm(k, shape, fan_in):
        return jax.random.normal(k, shape, jnp.float32) * fan_in ** -0.5

    def gain(k, shape):
        return 1.0 + 0.02 * jax.random.normal(k, shape, jnp.float32)

    def small(k, shape):
        return 0.01 * jax.random.normal(k, shape, jnp.float32)

    return {
        "x": jax.random.normal(ks[0], (BATCH, SEQ, D), jnp.float32),
        "p": jax.random.normal(ks[1], (DEPTH, BATCH, SEQ, PLE_DIM), jnp.float32),
        "g_mix": gain(ks[2], (L, D)),
        "w_in": nrm(ks[3], (L, D, IN_COLS), D),
        "cmp_pos_k": 0.02 * jax.random.normal(ks[4], (L, CMP_BLOCK, dh), jnp.float32),
        "cmp_w1_k": nrm(ks[5], (L, CMP_BLOCK * dh, CMP_HIDDEN), CMP_BLOCK * dh),
        "cmp_b1_k": small(ks[6], (L, CMP_HIDDEN)),
        "cmp_w2_k": nrm(ks[7], (L, CMP_HIDDEN, dh), CMP_HIDDEN),
        "cmp_pos_v": 0.02 * jax.random.normal(ks[8], (L, CMP_BLOCK, dh), jnp.float32),
        "cmp_w1_v": nrm(ks[9], (L, CMP_BLOCK * dh, CMP_HIDDEN), CMP_BLOCK * dh),
        "cmp_b1_v": small(ks[10], (L, CMP_HIDDEN)),
        "cmp_w2_v": nrm(ks[11], (L, CMP_HIDDEN, dh), CMP_HIDDEN),
        "w_branch_a": nrm(ks[12], (L, A_WIDTH, D), A_WIDTH),
        "w_branch_b": nrm(ks[13], (L, B_WIDTH, D), B_WIDTH),
        "w_out": nrm(ks[14], (L, D, D), D),
        "g_ffn": gain(ks[15], (L, D)),
        "w_router": nrm(ks[16], (L, D, N_EXPERTS), D),
        "router_bias": small(ks[17], (L, N_EXPERTS)),
        "w_gate": nrm(ks[18], (L, N_EXPERTS, D, EXPERT_HIDDEN), D),
        "w_up": nrm(ks[19], (L, N_EXPERTS, D, EXPERT_HIDDEN), D),
        "w_down": nrm(ks[20], (L, N_EXPERTS, EXPERT_HIDDEN, D), EXPERT_HIDDEN),
        "ws_gate": nrm(ks[21], (L, D, SHARED_HIDDEN), D),
        "ws_up": nrm(ks[22], (L, D, SHARED_HIDDEN), D),
        "ws_down": nrm(ks[23], (L, SHARED_HIDDEN, D), SHARED_HIDDEN),
        "g_ple": gain(ks[24], (L, D)),
        "w_ple_gate": nrm(ks[25], (L, D, D), D),
        "w_ple": nrm(ks[26], (L, PLE_DIM, D), PLE_DIM),
        "g_final": gain(ks[27], (D,)),
    }

def reference(x, p, g_mix, w_in, cmp_pos_k, cmp_w1_k, cmp_b1_k, cmp_w2_k, cmp_pos_v, cmp_w1_v, cmp_b1_v, cmp_w2_v, w_branch_a, w_branch_b, w_out, g_ffn, w_router, router_bias, w_gate, w_up, w_down, ws_gate, ws_up, ws_down, g_ple, w_ple_gate, w_ple, g_final):
    B, S, D = x.shape
    slopes = alibi_slopes(DIL_HEADS + NSA_HEADS)
    slopes_a = slopes[0::2]
    slopes_b = slopes[1::2]
    offsets = np.cumsum(IN_SIZES)[:-1].tolist()

    def heads(t, n):
        return t.reshape(B, S, n, HEAD_DIM)

    h = x
    for i in range(DEPTH):
        xn = rmsnorm(h, g_mix[i])
        proj = xn @ w_in[i]
        qa, ka, va, qb, kc_raw, vc_raw, k_slc, v_slc, k_win, v_win, g_nsa, g_a, g_b = jnp.split(proj, offsets, axis=-1)
        y_a = dilated_attention(heads(qa, DIL_HEADS), heads(ka, DIL_HEADS), heads(va, DIL_HEADS), slopes_a)
        kc = compress_blocks(heads(kc_raw, NSA_KV_HEADS), cmp_pos_k[i], cmp_w1_k[i], cmp_b1_k[i], cmp_w2_k[i])
        vc = compress_blocks(heads(vc_raw, NSA_KV_HEADS), cmp_pos_v[i], cmp_w1_v[i], cmp_b1_v[i], cmp_w2_v[i])
        gates = jax.nn.sigmoid(g_nsa).reshape(B, S, 3, NSA_HEADS)
        y_b = nsa_attention(heads(qb, NSA_HEADS), kc, vc, heads(k_slc, NSA_KV_HEADS), heads(v_slc, NSA_KV_HEADS),
                            heads(k_win, NSA_KV_HEADS), heads(v_win, NSA_KV_HEADS), gates, slopes_b)
        merged = (jax.nn.sigmoid(g_a) * (y_a.reshape(B, S, A_WIDTH) @ w_branch_a[i])
                  + jax.nn.sigmoid(g_b) * (y_b.reshape(B, S, B_WIDTH) @ w_branch_b[i]))
        h = h + merged @ w_out[i]
        h = h + moe_ffn(rmsnorm(h, g_ffn[i]), w_router[i], router_bias[i], w_gate[i], w_up[i], w_down[i],
                        ws_gate[i], ws_up[i], ws_down[i])
        h = h + (p[i] @ w_ple[i]) * jax.nn.sigmoid(rmsnorm(h, g_ple[i]) @ w_ple_gate[i])
    return rmsnorm(h, g_final)


_drawn_inputs = setup_inputs


def setup_inputs(seed=0):
    import zlib

    import numpy as np

    out = dict(_drawn_inputs(seed))
    spreads = {}
    factors = {'cmp_pos_k': 7.343,
     'cmp_b1_k': 33.107,
     'cmp_b1_v': 3.379,
     'g_ple': 46.635,
     'g_final': 9.696}
    for name, (base, spread) in spreads.items():
        noise = np.random.default_rng([zlib.crc32(name.encode()), seed]).standard_normal(out[name].shape)
        drawn = base * np.exp(spread * noise) if base else spread * noise
        out[name] = jnp.asarray(drawn.astype(out[name].dtype))
    for name, factor in factors.items():
        out[name] = (out[name] * factor).astype(out[name].dtype)
    return out
```

```python
from contextlib import ExitStack

import numpy as np

import concourse.bass as bass
from concourse import mybir

F32 = mybir.dt.float32
I32 = mybir.dt.int32
ALU = mybir.AluOpType
ACT = mybir.ActivationFunctionType
AX_X = mybir.AxisListType.X

P = 128
S = 512
D = 1024
NT = S // P
KD = D // P
DH = 64
NH = 8
PLE = 256
EPS = 1e-6
BIG = 1e30
WIDTH_A = NH * DH
COL_QA, COL_KA, COL_VA, COL_QB = 0, WIDTH_A, 2 * WIDTH_A, 3 * WIDTH_A
COL_KCR = 4 * WIDTH_A
COL_VCR, COL_KS, COL_VS, COL_KW, COL_VW, COL_GN = (COL_KCR + 128 * i for i in range(1, 7))
COL_GA = COL_GN + 3 * NH
COL_GB = COL_GA + D
CMP_STRIDE, CMP_BLOCK = 16, 32
NC = S // CMP_STRIDE - 1
NE = 64
NG = 8
EH = 256
CAP = 128
ROUTED_SCALE = 2.5
NOV = (S * 8 - NE) // CAP
NPAD = 2


def constants():
    p = np.arange(P)[:, None].astype(np.float64)
    c = np.arange(S)[None, :]
    dist = p + (S - P) - c
    count = ((dist >= 0) & (dist <= 128)).astype(int) + ((dist >= 0) & (dist % 4 == 0)) + ((dist >= 0) & (dist % 16 == 0))
    mdil = np.where(count > 0, -np.log(np.maximum(count, 1)), BIG)
    mfull = np.where(dist >= 0, 0.0, BIG)
    tok = (np.arange(NT)[None, :, None] * P + p[:, :, None])
    dcmp = tok - (np.arange(NC)[None, None, :] * CMP_STRIDE + CMP_BLOCK - 1)
    mcmp = np.where(dcmp >= 0, 0.0, BIG)
    slopes = 2.0 ** (-8.0 * np.arange(1, 2 * NH + 1) / (2 * NH))
    row = lambda v: np.broadcast_to(np.asarray(v, np.float64).reshape(1, -1), (P, np.asarray(v).size))
    e = np.arange(NE)
    tri64 = np.zeros((P, NE))
    tri64[:NE] = e[:, None] < e[None, :]
    g = np.arange(NG)
    parts = [
        ("ident", np.eye(P)),
        ("slot", row(np.arange(CAP))),
        ("tri", p < np.arange(P)[None, :]),
        ("ones", np.ones((P, P))),
        ("dist", dist),
        ("mdil", mdil),
        ("mfull", mfull),
        ("dcmp", dcmp.reshape(P, -1)),
        ("mcmp", mcmp.reshape(P, -1)),
        ("slopes_a", row(slopes[0::2])),
        ("slopes_b", row(slopes[1::2])),
        ("tok", p + P * np.arange(NT)[None, :] - S),
        ("tok8", 8 * (p + P * np.arange(NT)[None, :] - S) - 1),
        ("tri64", tri64),
        ("before8", row((g[:, None] > g[None, :]).astype(float))),
        ("tile", row(np.arange(NOV))),
        ("nhalf", row([-0.5] * NT)),
    ]
    place, at = {}, 0
    for name, a in parts:
        place[name] = (at, a.shape[1])
        at += a.shape[1]
    return np.ascontiguousarray(np.concatenate([a for _, a in parts], axis=1).astype(np.float32)), place


def build(nc, a, dbg=None):
    dbg = dbg or {}
    place = constants()[1]
    ncst = sum(n for _, n in place.values())
    xn2_d = nc.dram_tensor("xn2_rows", (S, D), F32, kind="Internal").ap()
    rows_d = nc.dram_tensor("expert_rows", (S * 8, D), F32, kind="Internal").ap()

    ctx = ExitStack()
    with ctx:
        def sb(name, shape, dt=F32):
            return ctx.enter_context(nc.sbuf_tensor("sb_" + name, shape, dt))

        def ps(name, shape, dt=F32):
            return ctx.enter_context(nc.psum_tensor(name, shape, dt))

        def sem(name):
            return ctx.enter_context(nc.semaphore(name))

        cst = sb("cst", [P, ncst])
        C = {k: cst[:, o:o + n] for k, (o, n) in place.items()}
        ident = C["ident"]
        h = sb("h", [P, NT, D])
        y = sb("y", [P, NT, D])
        gateT = sb("gateT", [P, 2 * KD, S])
        r1 = sb("r1", [P, 6144])
        work = sb("work", [P, 7152])
        small = sb("small", [P, 448])
        front = ExitStack()
        ctx.enter_context(front)
        xnT = front.enter_context(nc.sbuf_tensor("sb_xnT", [P, KD, S], F32))
        r2 = front.enter_context(nc.sbuf_tensor("sb_r2", [P, 8192], F32))
        r3 = front.enter_context(nc.sbuf_tensor("sb_r3", [P, 8192], F32))
        bank = [ps(f"bank{i}", [P, 512]) for i in range(8)]

        def psv(i, *shape):
            n = int(np.prod(shape))
            v = bank[i][:, 0:n]
            if len(shape) == 2:
                return v.rearrange("p (a b) -> p a b", a=shape[0])
            return v

        def chunks(ap):
            return ap.rearrange("(k p) n -> p k n", p=P)

        w_in = chunks(a["w_in"][0])

        s_cst, s_x, s_g = sem("s_cst"), [sem(f"s_x{t}") for t in range(NT)], sem("s_g")

        wA = r1[:, 0:3072].rearrange("p (i k n) -> p i k n", i=3, k=KD)
        wfA = r1[:, 3072:5120].rearrange("p (k n) -> p k n", k=KD)
        gn_w = r2[:, 0:192].rearrange("p (k n) -> p k n", k=KD)
        s_wA = [sem(f"s_wA{i}") for i in range(3)]
        s_wf, s_gn = sem("s_wf"), sem("s_gn")
        gates = small[:, 0:96].rearrange("p (t n) -> p t n", t=NT)
        gbc = r3[:, 0:D]
        ms, rr = small[:, 96:100], small[:, 100:104]

        def load_norm_gain(eng, dst, src, s):
            eng.dma_start(dst, src.partition_broadcast(P)).then_inc(s, 16)

        def norm_sums(dve, t, src, junk, msum):
            return nc.vector.tensor_tensor_reduce(out=junk, in0=src, in1=src, scale=1.0 / D, scalar=EPS,
                                                  op0=ALU.mult, op1=ALU.add, accum_out=msum[:, t:t + 1])

        s_ms, s_rr, s_xn, s_tp, s_tc, s_ng, s_nsa = map(sem, "s_ms s_rr s_xn s_tp s_tc s_ng s_nsa".split())
        with nc.Block() as block:
            @block.sync
            def _(sp):
                for t in range(NT):
                    sp.dma_start(h[:, t, :], a["x"][0, t * P:(t + 1) * P, :]).then_inc(s_x[t], 16)
                sp.dma_start(cst[:, :], a["cst"]).then_inc(s_cst, 16)
                sp.dma_start(gn_w, w_in[:, :, COL_GN:COL_GN + 24]).then_inc(s_gn, 16)
                for i, col in enumerate((COL_QA, COL_KA, COL_VA)):
                    sp.dma_start(wA[:, i], w_in[:, :, col:col + P]).then_inc(s_wA[i], 16)
                sp.dma_start(wfA, w_in[:, :, COL_GA:COL_GA + 256]).then_inc(s_wf, 16)

            @block.gpsimd
            def _(pool):
                load_norm_gain(pool, gbc, a["g_mix"][0], s_g)
                pool.wait_ge(s_cst, 16)
                for t in range(NT):
                    pool.wait_ge(s_ms, t + 1)
                    nc.gpsimd.tensor_tensor(rr[:, t:t + 1], ms[:, t:t + 1], C["nhalf"][:, 0:1], ALU.pow).then_inc(s_rr, 1)

            @block.vector
            def _(dve):
                for t in range(NT):
                    dve.wait_ge(s_x[t], 16)
                    norm_sums(dve, t, h[:, t, :], y[:, t, :], ms).then_inc(s_ms, 1)
                dve.wait_ge(s_g, 16)
                for t in range(NT):
                    dve.wait_ge(s_rr, t + 1)
                    nc.vector.scalar_tensor_tensor(out=y[:, t, :], in0=h[:, t, :], scalar=rr[:, t:t + 1], in1=gbc,
                                                   op0=ALU.mult, op1=ALU.mult).then_inc(s_xn, 1)
                for k in range(0, KD, 2):
                    dve.wait_ge(s_tp, k + 1)
                    nc.vector.tensor_copy(xnT[:, k, :], bank[k][:, :]).then_inc(s_tc, 1)

            @block.tensor
            def _(pe):
                pe.wait_ge(s_cst, 16)
                pe.wait_ge(s_xn, NT)
                for k in range(KD):
                    for t in range(NT):
                        last = nc.tensor.transpose(bank[k][:, t * P:(t + 1) * P], y[:, t, k * P:(k + 1) * P], ident)
                    last.then_inc(s_tp, 1)
                pe.wait_ge(s_tc, KD // 2)
                pe.wait_ge(s_ng, KD // 2)
                pe.wait_ge(s_gn, 16)
                for t in range(NT):
                    for k in range(KD):
                        last = nc.tensor.matmul(bank[0][:, t * 24:(t + 1) * 24], xnT[:, k, t * P:(t + 1) * P],
                                                gn_w[:, k, :], start=k == 0, stop=k == KD - 1)
                last.then_inc(s_nsa, 1)

            @block.scalar
            def _(act):
                for k in range(1, KD, 2):
                    act.wait_ge(s_tp, k + 1)
                    nc.scalar.copy(xnT[:, k, :], bank[k][:, :]).then_inc(s_ng, 1)
                act.wait_ge(s_nsa, 1)
                nc.scalar.activation(gates, psv(0, NT, 24), ACT.Sigmoid)

        if "xnT" in dbg:
            dump(nc, sem("d1"), dbg["xnT"], xnT[:, :, :])

        wBk = r2[:, 0:4096].rearrange("p (i k two n) -> p i k two n", i=4, k=KD, two=2)
        wBq = r2[:, 4096:6144].rearrange("p (k n) -> p k n", k=KD)
        wBv = r2[:, 6144:7168].rearrange("p (k i n) -> p k i n", k=KD, i=2)
        wfB = r1[:, 0:4096].rearrange("p (k n) -> p k n", k=KD)
        w1 = r3[:, 0:8192].rearrange("p (i t n) -> p i t n", i=2, t=16)
        w2 = r1[:, 5120:5504].rearrange("p (c n) -> p c n", c=2)
        b1c = small[:, 104:108]
        pos_rows = r1[0:32, 5504:5632]
        pos2 = small[:, 108:140]
        rowsum = small[:, 140:148]
        rsum3 = small[:, 148:154].rearrange("p (b i) -> p b i", b=2)
        coef = small[:, 436:444]
        minus_max = small[:, 158:160]
        slope2 = small[:, 160:164]
        gts = small[:, 164:212].rearrange("p (t b n) -> p t b n", t=NT, b=3)
        vc_sb = small[:, 212:276]
        kcT = small[:, 276:308]
        hTc = small[:, 308:436].rearrange("p (i c n) -> p i c n", i=2, c=2)

        qT = work[:, 0:1024].rearrange("p (i n) -> p i n", i=2)
        kT = work[:, 1024:2048].rearrange("p (i n) -> p i n", i=2)
        vv = work[:, 2048:2560].rearrange("p (t n) -> p t n", t=NT)
        bias = work[:, 2560:4608].rearrange("p (i n) -> p i n", i=4)
        bias_c = work[:, 4608:5104].rearrange("p (i t n) -> p i t n", i=4, t=NT)
        sc = work[:, 5104:6128].rearrange("p (i n) -> p i n", i=2)
        pT = work[:, 6128:7152].rearrange("p (i n) -> p i n", i=2)

        names = "projected evicted scored biased exped transposed copied pv_done y_done f_done f_evicted"
        A = {n: sem("a_" + n) for n in names.split()}
        B = {n: sem("b_" + n) for n in names.split()}
        s_tick = sem("s_tick")
        s_hid, s_gelu = sem("s_hid"), sem("s_gelu")
        ysum = r1[:, 5632:5888].rearrange("p (b i n) -> p b i n", b=2, i=2)
        wo = r2[:, 0:8192].rearrange("p (k n) -> p k n", k=KD)
        wm = r3[:, 0:8192].rearrange("p (i k n) -> p i k n", i=2, k=4)
        s_wB, s_w1, s_w2, s_pos, s_posT, s_posc = sem("s_wB"), sem("s_w1"), sem("s_w2"), sem("s_pos"), sem("s_posT"), sem("s_posc")
        s_wfB, s_wm, s_wo = sem("s_wfB"), sem("s_wm"), sem("s_wo")
        BS, BT, BV, BJ, BF = (0, 1), 2, (3, 4), (5, 6), 7

        unitsA = [dict(q=(hh, 0), rows=64 * hh, qt=qt, n=P * (qt + 1), k=0, bias=("a", hh), v=hh, group=hh * NT + qt, br=0)
                  for hh in range(2) for qt in range(NT)]
        unitsB = []
        for pr in range(2):
            for hh in range(2):
                for qt in range(NT):
                    for br in range(3):
                        unitsB.append(dict(q=(hh, pr), rows=64 * hh, qt=qt, n=NC if br == 0 else P * (qt + 1), k=br - 1,
                                           bias=("c" if br == 0 else "a", 2 * pr + hh), v=br - 1,
                                           group=(pr * 2 + hh) * NT + qt, br=br))
        fillA = {w: (2 * w, 2 * w + 2) for w in range(8)}
        fillB, n = {}, 0
        for w in range(48):
            if w % 3 != 0:
                fillB[w] = (n, n + 1)
                n += 1

        def n_chunks(u):
            return 1 if u["n"] == NC else u["n"] // P

        def unit_products(pe, u, w, it, per, s):
            rows = slice(u["rows"], u["rows"] + 64)
            lhsT = qT[rows, u["q"][1], u["qt"] * P:(u["qt"] + 1) * P]
            rhs = kcT[rows, 0:NC] if u["n"] == NC else kT[rows, u["k"], 0:u["n"]]
            nc.tensor.matmul(bank[BS[w % 2]][:, 0:u["n"]], lhsT, rhs, start=True, stop=True).then_inc(s["scored"], 1)

        def unit_transposes(pe, u, w, it, per, s):
            pe.wait_ge(s["exped"], it * per + w + 1)
            for j in range(n_chunks(u)):
                m = min(P, u["n"])
                last = nc.tensor.transpose(bank[BT][0:m, j * P:(j + 1) * P], sc[:, w % 2, j * P:j * P + m], ident)
            last.then_inc(s["transposed"], 1)

        def unit_values(pe, u, w, it, per, s, groups):
            pe.wait_ge(s["copied"], it * per + w + 1)
            if u["br"] == 0:
                pe.wait_ge(s["y_done"], it * groups + u["group"] + 1)
            out = bank[BV[u["group"] % 2]][:, u["br"] * DH:(u["br"] + 1) * DH]
            nch = n_chunks(u)
            for j in range(nch):
                m = min(P, u["n"])
                rhs = vc_sb[0:NC, :] if u["n"] == NC else vv[:, j, u["v"] * DH:(u["v"] + 1) * DH]
                last = nc.tensor.matmul(out, pT[0:m, w % 2, j * P:(j + 1) * P], rhs, start=j == 0, stop=j == nch - 1)
            last.then_inc(s["pv_done"], 1)

        def filler(pe, lo, hi, it, nchunk, wf, s, s_wload):
            for m in range(lo, hi):
                c, k = divmod(m, KD)
                if k == 0:
                    if c == 0:
                        pe.wait_ge(s_wload, 16 * it + 16)
                    pe.wait_ge(s["f_evicted"], it * nchunk + c + 1)
                last = nc.tensor.matmul(bank[BF][:, :], wf[:, k, c * P:(c + 1) * P], xnT[:, k, :],
                                        start=k == 0, stop=k == KD - 1)
                if k == KD - 1:
                    last.then_inc(s["f_done"], 1)

        def attend_pe(pe, units, fill, it, groups, nchunk, wf, s, s_wload):
            per = len(units)
            unit_products(pe, units[0], 0, it, per, s)
            for w, u in enumerate(units):
                if w + 1 < per:
                    unit_products(pe, units[w + 1], w + 1, it, per, s)
                if w in fill:
                    filler(pe, *fill[w], it, nchunk, wf, s, s_wload)
                if w:
                    unit_values(pe, units[w - 1], w - 1, it, per, s, groups)
                unit_transposes(pe, u, w, it, per, s)
            unit_values(pe, units[-1], per - 1, it, per, s, groups)

        def unit_bias(dve, u, w, it, per, s):
            dve.wait_ge(s["scored"], it * per + w + 1)
            dve.sem_inc(s_tick, 1)
            b = bias_c[:, u["bias"][1], u["qt"], :] if u["n"] == NC else bias[:, u["bias"][1], S - u["n"]:S]
            nc.vector.tensor_tensor_reduce(out=sc[:, w % 2, 0:u["n"]], in0=bank[BS[w % 2]][:, 0:u["n"]], in1=b,
                                           scale=1.0, scalar=0.1 * BIG, op0=ALU.add, op1=ALU.min,
                                           accum_out=minus_max[:, w % 2:w % 2 + 1]).then_inc(s["biased"], 1)

        def unit_exp(act, u, w, it, per, s, sums):
            act.wait_ge(s["biased"], it * per + w + 1)
            nc.scalar.activation(sc[:, w % 2, 0:u["n"]], sc[:, w % 2, 0:u["n"]], ACT.Exp, scale=-1.0,
                                 bias=minus_max[:, w % 2:w % 2 + 1], accum_out=sums).then_inc(s["exped"], 1)

        def unit_copy(act, u, w, it, per, s):
            act.wait_ge(s["transposed"], it * per + w + 1)
            m, n = min(P, u["n"]), P * n_chunks(u)
            nc.scalar.copy(pT[0:m, w % 2, 0:n], bank[BT][0:m, 0:n]).then_inc(s["copied"], 1)

        def attend_act(act, units, it, s, sums):
            per = len(units)
            for w, u in enumerate(units):
                unit_exp(act, u, w, it, per, s, sums(u, w))
                unit_copy(act, u, w, it, per, s)

        def attend_dve(dve, units, fill, it, nchunk, s, put, gate_at):
            per = len(units)
            unit_bias(dve, units[0], 0, it, per, s)
            for w, u in enumerate(units):
                if w + 1 < per:
                    unit_bias(dve, units[w + 1], w + 1, it, per, s)
                if w in fill and fill[w][1] % KD == 0:
                    c = fill[w][1] // KD - 1
                    dve.wait_ge(s["f_done"], it * nchunk + c + 1)
                    nc.vector.tensor_copy(gate_at(c), bank[BF][:, :]).then_inc(s["f_evicted"], 1)
                if w and (w - 1 == per - 1 or units[w]["group"] != units[w - 1]["group"]):
                    put(dve, units[w - 1], w - 1)
            put(dve, units[-1], per - 1)

        with nc.Block() as block:
            @block.sync
            def _(sp):
                sp.dma_start(w2[:, :, 0:DH], a["cmp_w2_k"][0].rearrange("(c p) n -> p c n", p=P)).then_inc(s_w2, 16)
                sp.dma_start(w2[:, :, DH:2 * DH], a["cmp_w2_k"][0].rearrange("(c p) n -> p c n", p=P)).then_inc(s_w2, 16)
                sp.dma_start(w2[:, :, 2 * DH:3 * DH], a["cmp_w2_v"][0].rearrange("(c p) n -> p c n", p=P)).then_inc(s_w2, 16)
                for i, n in enumerate("kv"):
                    sp.dma_start(b1c[:, 2 * i:2 * i + 2], a["cmp_b1_" + n][0].rearrange("(c p) -> p c", p=P),
                                 allow_slow_non_contiguous=True).then_inc(s_w2, 16)
                    sp.dma_start(pos_rows[16 * i:16 * i + 16, :],
                                 a["cmp_pos_" + n][0].rearrange("(t two) d -> t (two d)", two=2)).then_inc(s_pos, 16)
                with sp.Fori(1, 4) as it:
                    sp.wait_ge(A["projected"], 3 * it)
                    for i, col in enumerate((COL_QA, COL_KA, COL_VA)):
                        sp.dma_start(wA[:, i], w_in[:, :, bass.ds(it * P + col, P)]).then_inc(s_wA[i], 16)
                    sp.wait_ge(A["f_done"], 2 * it)
                    sp.dma_start(wfA, w_in[:, :, bass.ds(it * 256 + COL_GA, 256)]).then_inc(s_wf, 16)
                for i, n in enumerate("kv"):
                    sp.dma_start(w1[:, i], a["cmp_w1_" + n][0].rearrange("(t p) n -> p t n", p=P)).then_inc(s_w1, 16)
                load_b_group(sp, w_in, wBk, wBq, wBv, 0, s_wB)
                sp.wait_ge(A["projected"], 12)
                sp.wait_ge(A["f_done"], 8)
                sp.dma_start(wfB, w_in[:, :, COL_GB:COL_GB + 512]).then_inc(s_wfB, 16)

            @block.tensor
            def _(pe):
                pe.wait_ge(s_pos, 32)
                nc.tensor.transpose(bank[BT][:, 0:32], pos_rows, ident[0:32, 0:32]).then_inc(s_posT, 1)
                pe.wait_ge(s_posc, 1)
                with pe.Fori(0, 4) as it:
                    for i in range(2):
                        pe.wait_ge(s_wA[i], 16 * it + 16)
                        pe.wait_ge(A["evicted"], 3 * it + 1)
                        for k in range(KD):
                            last = nc.tensor.matmul(bank[BJ[i]][:, :], wA[:, i, k, :], xnT[:, k, :],
                                                    start=k == 0, stop=k == KD - 1)
                        last.then_inc(A["projected"], 1)
                    pe.wait_ge(s_wA[2], 16 * it + 16)
                    pe.wait_ge(A["evicted"], 3 * it + 2)
                    for t in range(NT):
                        for k in range(KD):
                            last = nc.tensor.matmul(bank[BJ[0]][:, t * P:(t + 1) * P], xnT[:, k, t * P:(t + 1) * P],
                                                    wA[:, 2, k, :], start=k == 0, stop=k == KD - 1)
                    last.then_inc(A["projected"], 1)
                    pe.wait_ge(A["evicted"], 3 * it + 4)
                    attend_pe(pe, unitsA, fillA, it, 8, 2, wfA, A, s_wf)

            @block.vector
            def _(dve):
                dve.wait_ge(s_posT, 1)
                nc.vector.tensor_copy(pos2, bank[BT][:, 0:32]).then_inc(s_posc, 1)
                dve.sem_inc(A["evicted"], 1)
                dve.sem_inc(A["f_evicted"], 1)
                dve.sem_inc(A["y_done"], 2)
                with dve.Fori(0, 4) as it:
                    nc.vector.tensor_copy(slope2[:, 0:2], C["slopes_a"][:, bass.ds(it * 2, 2)])
                    dve.drain()
                    for hh in range(2):
                        nc.vector.scalar_tensor_tensor(out=bias[:, hh, :], in0=C["dist"], scalar=slope2[:, hh:hh + 1],
                                                       in1=C["mdil"], op0=ALU.mult, op1=ALU.add)
                    dve.wait_ge(A["projected"], 3 * it + 1)
                    nc.vector.tensor_scalar(qT[:, 0, :], bank[BJ[0]][:, :], -(DH ** -0.5), None, ALU.mult).then_inc(A["evicted"], 1)
                    dve.wait_ge(A["projected"], 3 * it + 2)
                    nc.vector.tensor_copy(kT[:, 0, :], bank[BJ[1]][:, :]).then_inc(A["evicted"], 1)
                    dve.wait_ge(A["projected"], 3 * it + 3)
                    nc.vector.tensor_copy(vv, psv(BJ[0], NT, P)).then_inc(A["evicted"], 1)
                    dve.drain()

                    def put(dve, u, w):
                        dve.wait_ge(A["pv_done"], it * 8 + w + 1)
                        nc.vector.reciprocal(coef[:, w:w + 1], rowsum[:, w:w + 1])
                        dve.drain()
                        nc.vector.tensor_scalar(y[:, u["qt"], bass.ds(it * P + u["v"] * DH, DH)],
                                                bank[BV[u["group"] % 2]][:, 0:DH], coef[:, w:w + 1], None,
                                                ALU.mult).then_inc(A["y_done"], 1)

                    attend_dve(dve, unitsA, fillA, it, 2, A, put, lambda c: gateT[:, it * 2 + c, :])

            @block.scalar
            def _(act):
                with act.Fori(0, 4) as it:
                    attend_act(act, unitsA, it, A, lambda u, w: rowsum[:, w:w + 1])

        if "ya" in dbg:
            dump(nc, sem("d2"), dbg["ya"], y[:, :, 0:512])


        def blocks_of(i, half):
            return y[:, 2 * i + half, 768:768 + 8 * NC].rearrange("p (t n) -> p t n", t=8)

        with nc.Block() as block:
            @block.sync
            def _(sp):
                sp.wait_ge(B["projected"], 9)
                load_b_group(sp, w_in, wBk, wBq, wBv, 1, s_wB)
                sp.wait_ge(B["f_done"], 4)
                sp.dma_start(wfB, w_in[:, :, COL_GB + 512:COL_GB + 1024]).then_inc(s_wfB, 16)
                sp.wait_ge(B["projected"], 18)
                sp.dma_start(wo, chunks(a["w_out"][0])).then_inc(s_wo, 16)
                for i, n in enumerate("ab"):
                    sp.dma_start(wm[:, i], a["w_branch_" + n][0].rearrange("(k p) n -> p k n", p=P)).then_inc(s_wm, 16)

            @block.tensor
            def _(pe):
                pe.wait_ge(s_w1, 32)
                pe.wait_ge(s_w2, 80)
                with pe.Fori(0, 2) as it:
                    pe.wait_ge(s_wB, 11 * 16 * it + 11 * 16)
                    for i in range(4):
                        pe.wait_ge(B["evicted"], 9 * it + max(i - 1, 0) + 1)
                        for k in range(KD):
                            last = nc.tensor.matmul(bank[BJ[i % 2]][:, :], wBk[:, i, k], xnT[:, k, :],
                                                    start=k == 0, stop=k == KD - 1)
                        last.then_inc(B["projected"], 1)
                    pe.wait_ge(B["evicted"], 9 * it + 4)
                    for t in range(NT):
                        for k in range(KD):
                            last = nc.tensor.matmul(bank[BJ[0]][:, t * P:(t + 1) * P], xnT[:, k, t * P:(t + 1) * P],
                                                    wBv[:, k], start=k == 0, stop=k == KD - 1)
                    last.then_inc(B["projected"], 1)
                    for pr in range(2):
                        pe.wait_ge(B["evicted"], 9 * it + 5 + pr)
                        for k in range(KD):
                            last = nc.tensor.matmul(bank[BJ[1 - pr]][:, :], wBq[:, k, pr * P:(pr + 1) * P], xnT[:, k, :],
                                                    start=k == 0, stop=k == KD - 1)
                        last.then_inc(B["projected"], 1)
                    for i in range(2):
                        pe.wait_ge(B["evicted"], 9 * it + 7 + i)
                        for c in range(2):
                            for t in range(16):
                                last = nc.tensor.matmul(bank[BJ[1 - i]][:, c * 32:c * 32 + NC], w1[:, i, t, c * P:(c + 1) * P],
                                                        blocks_of(i, t // 8)[:, t % 8, :], start=t == 0, stop=t == 15)
                        last.then_inc(s_hid, 1)
                    pe.wait_ge(s_gelu, 4 * it + 2)
                    for c in range(2):
                        last = nc.tensor.matmul(bank[BJ[1]][:, 0:NC], w2[:, c, 0:P], hTc[:, 0, c, 0:NC], start=c == 0, stop=c == 1)
                    last.then_inc(B["projected"], 1)
                    pe.wait_ge(s_gelu, 4 * it + 4)
                    for c in range(2):
                        last = nc.tensor.matmul(bank[BJ[0]][0:NC, 0:DH], hTc[:, 1, c, 0:NC], w2[:, c, P:P + DH], start=c == 0, stop=c == 1)
                    last.then_inc(B["projected"], 1)
                    pe.wait_ge(B["evicted"], 9 * it + 10)
                    attend_pe(pe, unitsB, fillB, it, 16, 4, wfB, B, s_wfB)

            @block.vector
            def _(dve):
                dve.sem_inc(B["evicted"], 1)
                dve.sem_inc(B["f_evicted"], 1)
                dve.sem_inc(B["y_done"], 2)
                with dve.Fori(0, 2) as it:
                    nc.vector.tensor_copy(slope2, C["slopes_b"][:, bass.ds(it * 4, 4)])
                    for b in range(3):
                        nc.vector.tensor_copy(gts[:, :, b, :], gates[:, :, bass.ds(it * 4 + b * NH, 4)])
                    dve.drain()
                    for i in range(4):
                        nc.vector.scalar_tensor_tensor(out=bias[:, i, :], in0=C["dist"], scalar=slope2[:, i:i + 1],
                                                       in1=C["mfull"], op0=ALU.mult, op1=ALU.add)
                        nc.vector.scalar_tensor_tensor(out=bias_c[:, i].rearrange("p t n -> p (t n)"), in0=C["dcmp"],
                                                       scalar=slope2[:, i:i + 1], in1=C["mcmp"], op0=ALU.mult, op1=ALU.add)
                    for i in range(2):
                        dve.wait_ge(B["projected"], 9 * it + i + 1)
                        nc.vector.tensor_copy(kT[:, i, :], bank[BJ[i]][:, :]).then_inc(B["evicted"], 1)
                    for i in range(2):
                        dve.wait_ge(B["projected"], 9 * it + 3 + i)
                        raw = bank[BJ[i]][:, :].rearrange("p (n t two) -> p two t n", t=8, two=2)
                        for half in range(2):
                            for par in range(2):
                                rows = slice(64 * par, 64 * par + 64)
                                pos = pos2[rows, 16 * i + 8 * half:16 * i + 8 * half + 8].unsqueeze(2).to_broadcast([64, 8, NC])
                                last = nc.vector.tensor_tensor(blocks_of(i, half)[rows], raw[rows, par, :, half:half + NC], pos, ALU.add)
                        last.then_inc(B["evicted"], 1)
                    dve.wait_ge(B["projected"], 9 * it + 5)
                    nc.vector.tensor_copy(vv, psv(BJ[0], NT, P)).then_inc(B["evicted"], 1)
                    for pr in range(2):
                        dve.wait_ge(B["projected"], 9 * it + 6 + pr)
                        nc.vector.tensor_scalar(qT[:, pr, :], bank[BJ[1 - pr]][:, :], -(DH ** -0.5), None, ALU.mult).then_inc(B["evicted"], 1)
                    dve.wait_ge(B["projected"], 9 * it + 8)
                    nc.vector.tensor_copy(kcT[:, 0:NC], bank[BJ[1]][:, 0:NC]).then_inc(B["evicted"], 1)
                    dve.wait_ge(B["projected"], 9 * it + 9)
                    nc.vector.tensor_copy(vc_sb[0:NC, :], bank[BJ[0]][0:NC, 0:DH]).then_inc(B["evicted"], 1)
                    dve.drain()

                    def put(dve, u, w):
                        head, b = u["group"] // NT, u["group"] % 2
                        c = coef[:, 4 * b:4 * b + 3]
                        bk = bank[BV[b]]
                        dve.wait_ge(B["pv_done"], it * 48 + w + 1)
                        nc.vector.tensor_scalar(c, rsum3[:, b, :], 0.5, None, ALU.max)
                        dve.drain()
                        nc.vector.reciprocal(c, c)
                        dve.drain()
                        nc.vector.tensor_tensor(c, c, gts[:, u["qt"], :, head], ALU.mult)
                        dve.drain()
                        dst = y[:, u["qt"], bass.ds(it * 4 * DH + WIDTH_A + head * DH, DH)]
                        nc.vector.tensor_scalar(ysum[:, b, 0, :], bk[:, 0:DH], c[:, 0:1], None, ALU.mult)
                        dve.drain()
                        nc.vector.scalar_tensor_tensor(out=ysum[:, b, 1, :], in0=bk[:, DH:2 * DH], scalar=c[:, 1:2],
                                                       in1=ysum[:, b, 0, :], op0=ALU.mult, op1=ALU.add)
                        dve.drain()
                        nc.vector.scalar_tensor_tensor(out=dst, in0=bk[:, 2 * DH:3 * DH], scalar=c[:, 2:3],
                                                       in1=ysum[:, b, 1, :], op0=ALU.mult, op1=ALU.add).then_inc(B["y_done"], 1)

                    attend_dve(dve, unitsB, fillB, it, 4, B, put, lambda c: gateT[:, it * 4 + KD + c, :])

            @block.scalar
            def _(act):
                with act.Fori(0, 2) as it:
                    for i in range(2):
                        act.wait_ge(s_hid, 2 * it + i + 1)
                        for c in range(2):
                            nc.scalar.activation(hTc[:, i, c, 0:NC], bank[BJ[1 - i]][:, c * 32:c * 32 + NC], ACT.Gelu_apprx_tanh,
                                                 bias=b1c[:, 2 * i + c:2 * i + c + 1]).then_inc(s_gelu, 1)
                    attend_act(act, unitsB, it, B, lambda u, w: rsum3[:, u["group"] % 2, u["br"]:u["br"] + 1])

        if "yb" in dbg:
            dump(nc, sem("d3"), dbg["yb"], y[:, :, 512:1024])

        mT = xnT
        yT = r1[:, 0:4096].rearrange("p (k n) -> p k n", k=KD)
        wsg = r3[:, 0:4096].rearrange("p (i k n) -> p i k n", i=2, k=KD)
        wsd = r3[:, 4096:6144].rearrange("p (c n) -> p c n", c=2)
        xn2T = gateT[:, 0:KD, :]
        wr = gateT[:, KD, 0:512].rearrange("p (k n) -> p k n", k=KD)
        rb = gateT[:, KD + 1, 0:NE]
        gbc2 = gateT[:, KD + 2:KD + 4, :].rearrange("p a b -> p (a b)")
        xpart = small[:, 96:104]
        NEP = NE + NPAD
        at = [0]

        def wk(n, *dims):
            v = work[:, at[0]:at[0] + n]
            at[0] += n
            if len(dims) == 2:
                return v.rearrange("p (a b) -> p a b", a=dims[0])
            if len(dims) == 3:
                return v.rearrange("p (a b c) -> p a b c", a=dims[0], b=dims[1])
            return v

        posm = wk(NEP * NT, NEP, NT)
        tokw = wk(NEP * NT * 3, NEP, NT, 3)
        wts = wk(NEP)
        dstf = wk(NEP)
        didx = wk(2).bitcast(I32)
        etab = wk(NOV).bitcast(I32)
        ntot = wk(1).bitcast(I32)
        q128 = wk(NOV)
        idx = wk(2).bitcast(I32)
        onehot = wk(NT * CAP, NT, CAP)
        sg, hid = wk(EH), wk(EH)
        hT = wk(2 * CAP, 2, CAP)
        at_moe = at[0]
        sco, sel, selm, rep, mask, wn, pos1 = (wk(NT * NE, NT, NE) for _ in range(7))
        g8 = wk(NT * NG * 8, NT * NG, 8)
        gs, gm, gneg, rank = (wk(NT * NG, NT, NG) for _ in range(4))
        m8 = wk(NT * 8, NT, 8)
        wsum = wk(NT)
        novT = wk(P)
        ovs, nov, oven = (wk(NE) for _ in range(3))
        rank2 = wk(NOV)
        assert at[0] <= 7152, at[0]
        big = gateT[:, KD + 4:KD + 8, :].rearrange("p a b -> p (a b)")
        pair = big[:, 0:NT * NG * NG].rearrange("p (t a b) -> p t a b", t=NT, a=NG)
        pair2 = big[:, 256:256 + NT * NG * NG].rearrange("p (t a b) -> p t a b", t=NT, a=NG)
        jcmp = big[:, 0:NOV * NE].rearrange("p (j e) -> p j e", j=NOV)
        shid = y

        cn = "yt_done yt_dve yt_act sig merged_pe merged wo_done h_done ms rr xn stored xt_done xt_dve xt_act r_done sco mask pos_pe posd cnt_pe nov ov_pe gu_done silu hid hT_pe hT dn_done dn_out".split()
        M = {n: sem("m_" + n) for n in cn}
        s_ws, s_wr, s_g2 = sem("s_ws"), sem("s_wr"), sem("s_g2")
        s_raw = [[sem(f"s_raw{b}_{n}") for n in ("gate", "up")] for b in range(2)]
        s_wd = [sem("s_wd0"), sem("s_wd1")]
        assert at_moe <= 7152 - 4096, at_moe
        raw = [v.rearrange("p (i n) -> p i n", i=2) for v in (r1[:, 0:4096], work[:, 7152 - 4096:7152])]
        xg = [r1[:, 4096 + b * D:4096 + (b + 1) * D] for b in range(2)]
        Wd = [y[:, 2 * b:2 * b + 2, :] for b in range(2)]

        def load_gu(sp, e, b, i):
            w = a[("w_gate", "w_up")[i]][0].rearrange("e (p k) n -> e p (k n)", k=KD)
            sp.dma_start(raw[b][:, i, :], w[e]).then_inc(s_raw[b][i], 16)

        with nc.Block() as block:
            @block.sync
            def _(sp):
                sp.wait_ge(M["merged"], KD)
                sp.dma_start(wr, chunks(a["w_router"][0])).then_inc(s_wr, 16)
                sp.dma_start(rb, a["router_bias"][0].partition_broadcast(P)).then_inc(s_wr, 16)
                sp.dma_start(gbc2, a["g_ffn"][0].partition_broadcast(P)).then_inc(s_g2, 16)
                for i, n in enumerate(("ws_gate", "ws_up")):
                    sp.dma_start(wsg[:, i], chunks(a[n][0])).then_inc(s_ws, 16)
                sp.dma_start(wsd, a["ws_down"][0].rearrange("(c p) n -> p c n", p=P)).then_inc(s_ws, 16)
                load_gu(sp, 0, 0, 0)
                load_gu(sp, 0, 0, 1)
                for t in range(NT):
                    sp.wait_ge(M["xn"], t + 1)
                    sp.dma_start(xn2_d[t * P:(t + 1) * P, :], y[:, t, :]).then_inc(M["stored"], 16)
                sp.wait_ge(M["stored"], 16 * NT)

            @block.gpsimd
            def _(pool):
                for t in range(NT):
                    pool.wait_ge(M["ms"], t + 1)
                    nc.gpsimd.tensor_tensor(xpart[:, 4 + t:5 + t], xpart[:, t:t + 1], C["nhalf"][:, 0:1], ALU.pow).then_inc(M["rr"], 1)

            @block.tensor
            def _(pe):
                for k in range(KD):
                    for t in range(NT):
                        last = nc.tensor.transpose(bank[k][:, t * P:(t + 1) * P], y[:, t, k * P:(k + 1) * P], ident)
                    last.then_inc(M["yt_done"], 1)
                pe.wait_ge(s_wm, 32)
                pe.wait_ge(M["yt_dve"], 4)
                pe.wait_ge(M["yt_act"], 4)
                for m in range(KD):
                    if m >= 4:
                        pe.wait_ge(M["merged"], m - 3)
                    for i in range(2):
                        for k in range(4):
                            last = nc.tensor.matmul(bank[2 * (m % 4) + i][:, :], wm[:, i, k, m * P:(m + 1) * P],
                                                    yT[:, 4 * i + k, :], start=k == 0, stop=k == 3)
                    last.then_inc(M["merged_pe"], 1)
                pe.wait_ge(s_wo, 16)
                pe.wait_ge(M["merged"], KD)

                def out_proj(t):
                    if t >= 2:
                        pe.wait_ge(M["h_done"], 2 * (t - 1))
                    for i in range(2):
                        for k in range(KD):
                            last = nc.tensor.matmul(bank[2 * (t % 2) + i][:, :], mT[:, k, t * P:(t + 1) * P],
                                                    wo[:, k, i * 512:(i + 1) * 512], start=k == 0, stop=k == KD - 1)
                    last.then_inc(M["wo_done"], 1)

                def transpose_xn(t):
                    pe.wait_ge(M["xn"], t + 1)
                    if t:
                        pe.wait_ge(M["xt_dve"], t)
                        pe.wait_ge(M["xt_act"], t)
                    for k in range(KD):
                        last = nc.tensor.transpose(bank[4 + k // 4][:, (k % 4) * P:(k % 4 + 1) * P],
                                                   y[:, t, k * P:(k + 1) * P], ident)
                    last.then_inc(M["xt_done"], 1)

                def router(t):
                    pe.wait_ge(M["xt_dve"], t + 1)
                    pe.wait_ge(M["xt_act"], t + 1)
                    for k in range(KD):
                        last = nc.tensor.matmul(bank[6][:, t * NE:(t + 1) * NE], xn2T[:, k, t * P:(t + 1) * P], wr[:, k, :],
                                                start=k == 0, stop=k == KD - 1)
                    last.then_inc(M["r_done"], 1)

                def shared_up(t):
                    for k in range(KD):
                        last = nc.tensor.matmul(bank[t][:, :], xn2T[:, k, t * P:(t + 1) * P], wsg[:, :, k, :],
                                                start=k == 0, stop=k == KD - 1)
                    last.then_inc(M["gu_done"], 1)

                out_proj(0)
                out_proj(1)
                transpose_xn(0)
                pe.wait_ge(s_wr, 32)
                router(0)
                out_proj(2)
                transpose_xn(1)
                router(1)
                out_proj(3)
                transpose_xn(2)
                router(2)
                pe.wait_ge(s_ws, 48)
                shared_up(0)
                transpose_xn(3)
                router(3)
                shared_up(1)
                pe.wait_ge(M["h_done"], 8)
                shared_up(2)
                pe.wait_ge(M["mask"], 1)
                for t in range(NT):
                    for u in range(t + 1):
                        last = nc.tensor.matmul(bank[7][:, t * NE:(t + 1) * NE], C["tri"] if u == t else C["ones"],
                                                mask[:, u, :], start=u == 0, stop=u == t)
                last.then_inc(M["pos_pe"], 1)
                pe.wait_ge(M["posd"], 1)
                for t in range(NT):
                    last = nc.tensor.matmul(bank[7][0:NE, 0:P], mask[:, t, :], C["ones"], start=t == 0, stop=t == NT - 1)
                last.then_inc(M["cnt_pe"], 1)
                shared_up(3)
                pe.wait_ge(M["nov"], 1)
                nc.tensor.matmul(bank[7][:, 128:128 + NE], novT[0:NE, :], C["tri64"][0:NE, :], start=True, stop=True)
                nc.tensor.matmul(bank[7][:, 256:256 + NE], novT[0:NE, :], ident[0:NE, 0:NE], start=True, stop=True).then_inc(M["ov_pe"], 1)
                for t in range(NT):
                    pe.wait_ge(M["hid"], t + 1)
                    for c in range(2):
                        last = nc.tensor.transpose(bank[4][:, c * P:(c + 1) * P], shid[:, t, c * P:(c + 1) * P], ident)
                    last.then_inc(M["hT_pe"], 1)
                    pe.wait_ge(M["hT"], t + 1)
                    if t >= 2:
                        pe.wait_ge(M["dn_out"], 2 * (t - 1))
                    for i in range(2):
                        for c in range(2):
                            last = nc.tensor.matmul(bank[5 + i if t % 2 == 0 else i][:, :], shid[:, t, 512 + c * P:512 + (c + 1) * P],
                                                    wsd[:, c, i * 512:(i + 1) * 512], start=c == 0, stop=c == 1)
                    last.then_inc(M["dn_done"], 1)

            @block.scalar
            def _(act):
                for k in range(1, KD, 2):
                    act.wait_ge(M["yt_done"], k + 1)
                    nc.scalar.copy(yT[:, k, :], bank[k][:, :]).then_inc(M["yt_act"], 1)
                for m in range(KD):
                    nc.scalar.activation(gateT[:, m, :], gateT[:, m, :], ACT.Sigmoid)
                    nc.scalar.activation(gateT[:, KD + m, :], gateT[:, KD + m, :], ACT.Sigmoid).then_inc(M["sig"], 1)
                for t in range(NT):
                    act.wait_ge(M["xt_done"], t + 1)
                    nc.scalar.copy(xn2T[:, 4:8, t * P:(t + 1) * P], psv(5, 4, P)).then_inc(M["xt_act"], 1)
                act.wait_ge(M["r_done"], NT)
                nc.scalar.activation(sco, psv(6, NT, NE), ACT.Sigmoid).then_inc(M["sco"], 1)
                act.wait_ge(M["stored"], 16 * NT)
                for t in range(NT):
                    act.wait_ge(M["gu_done"], t + 1)
                    nc.scalar.activation(shid[:, t, 256:512], bank[t][:, 0:EH], ACT.Silu).then_inc(M["silu"], 1)
                for t in range(NT):
                    act.wait_ge(M["hT_pe"], t + 1)
                    nc.scalar.copy(shid[:, t, 512:768], bank[4][:, 0:256]).then_inc(M["hT"], 1)

            @block.vector
            def _(dve):
                for k in range(0, KD, 2):
                    dve.wait_ge(M["yt_done"], k + 1)
                    nc.vector.tensor_copy(yT[:, k, :], bank[k][:, :]).then_inc(M["yt_dve"], 1)
                for m in range(KD):
                    dve.wait_ge(M["sig"], m + 1)
                    dve.wait_ge(M["merged_pe"], m + 1)
                    nc.vector.tensor_tensor(gateT[:, m, :], gateT[:, m, :], bank[2 * (m % 4)][:, :], ALU.mult)
                    nc.vector.tensor_tensor(gateT[:, KD + m, :], gateT[:, KD + m, :], bank[2 * (m % 4) + 1][:, :], ALU.mult)
                    dve.drain()
                    nc.vector.tensor_tensor(mT[:, m, :], gateT[:, m, :], gateT[:, KD + m, :], ALU.add).then_inc(M["merged"], 1)
                dve.wait_ge(s_g2, 16)
                for t in range(NT):
                    dve.wait_ge(M["wo_done"], t + 1)
                    for i in range(2):
                        hh = h[:, t, i * 512:(i + 1) * 512]
                        nc.vector.tensor_tensor(hh, hh, bank[2 * (t % 2) + i][:, :], ALU.add).then_inc(M["h_done"], 1)
                    dve.drain()
                    norm_sums(dve, t, h[:, t, :], y[:, t, :], xpart).then_inc(M["ms"], 1)
                    dve.wait_ge(M["rr"], t + 1)
                    nc.vector.scalar_tensor_tensor(out=y[:, t, :], in0=h[:, t, :], scalar=xpart[:, 4 + t:5 + t], in1=gbc2,
                                                   op0=ALU.mult, op1=ALU.mult).then_inc(M["xn"], 1)
                    dve.wait_ge(M["xt_done"], t + 1)
                    nc.vector.tensor_copy(xn2T[:, 0:4, t * P:(t + 1) * P], psv(4, 4, P)).then_inc(M["xt_dve"], 1)
                nc.vector.memset(posm[:, NE:NEP, :], -1.0)
                nc.vector.memset(tokw[:, NE:NEP], 0.0)
                nc.vector.tensor_copy(tokw[:, 0:NE, :, 0], C["tok"].unsqueeze(1).to_broadcast([P, NE, NT]))
                dve.wait_ge(M["sco"], 1)
                dve.wait_ge(s_wr, 32)
                nc.vector.tensor_tensor(sel, sco, rb.unsqueeze(1).to_broadcast([P, NT, NE]), ALU.add)
                dve.drain()
                for j in range(NT * NG):
                    nc.vector.max(g8[:, j, :], sel[:, j // NG, (j % NG) * 8:(j % NG + 1) * 8])
                dve.drain()
                gs_ = gs.rearrange("p t g -> p (t g)")
                nc.vector.tensor_tensor(gs_, g8[:, :, 0], g8[:, :, 1], ALU.add)
                dve.drain()
                mine = gs.unsqueeze(3).to_broadcast([P, NT, NG, NG])
                other = gs.unsqueeze(2).to_broadcast([P, NT, NG, NG])
                before = C["before8"].rearrange("p (a b) -> p a b", a=NG).unsqueeze(1).to_broadcast([P, NT, NG, NG])
                nc.vector.tensor_tensor(pair, other, mine, ALU.is_gt)
                nc.vector.tensor_tensor(pair2, other, mine, ALU.is_equal)
                dve.drain()
                nc.vector.tensor_tensor(pair2, pair2, before, ALU.mult)
                dve.drain()
                nc.vector.tensor_tensor(pair, pair, pair2, ALU.add)
                dve.drain()
                nc.vector.tensor_reduce(rank, pair, axis=AX_X, op=ALU.add)
                dve.drain()
                nc.vector.tensor_scalar(gm, rank, 4.0, None, ALU.is_lt)
                dve.drain()
                nc.vector.tensor_scalar(gneg, gm, 1.0, BIG, ALU.subtract, ALU.mult)
                each = lambda v: v.rearrange("p t g -> p (t g)").unsqueeze(2).to_broadcast([P, NT * NG, 8])
                flat8 = lambda v: v.rearrange("p t (g e) -> p (t g) e", g=NG)
                nc.vector.tensor_tensor(flat8(selm), flat8(sel), each(gm), ALU.mult)
                dve.drain()
                nc.vector.tensor_tensor(flat8(selm), flat8(selm), each(gneg), ALU.add)
                dve.drain()
                for t in range(NT):
                    nc.vector.max(m8[:, t, :], selm[:, t, :])
                dve.drain()
                for t in range(NT):
                    nc.vector.match_replace(out=rep[:, t, :], in_to_replace=m8[:, t, :], in_values=selm[:, t, :], imm_value=-2.0 * BIG)
                dve.drain()
                nc.vector.tensor_tensor(mask, rep, selm, ALU.not_equal).then_inc(M["mask"], 1)
                dve.drain()
                nc.vector.tensor_tensor(wn, sco, mask, ALU.mult)
                dve.drain()
                nc.vector.tensor_reduce(wsum, wn, axis=AX_X, op=ALU.add)
                dve.drain()
                nc.vector.reciprocal(wsum, wsum)
                dve.drain()
                nc.vector.tensor_scalar(wsum, wsum, ROUTED_SCALE, None, ALU.mult)
                dve.drain()
                nc.vector.tensor_tensor(tokw[:, 0:NE, :, 1].rearrange("p e t -> p t e"), wn,
                                        wsum.unsqueeze(2).to_broadcast([P, NT, NE]), ALU.mult)
                src, dst = mask, sel
                for n in (1, 2, 4, 8, 16, 32):
                    nc.vector.tensor_tensor(dst[:, :, n:NE], src[:, :, n:NE], src[:, :, 0:NE - n], ALU.add)
                    nc.vector.tensor_copy(dst[:, :, 0:n], src[:, :, 0:n])
                    dve.drain()
                    src, dst = dst, (selm if dst is sel else sel)
                nc.vector.tensor_tensor(src, src, C["tok8"].unsqueeze(2).to_broadcast([P, NT, NE]), ALU.add)
                dve.drain()
                nc.vector.tensor_copy(tokw[:, 0:NE, :, 2].rearrange("p e t -> p t e"), src)
                dve.wait_ge(M["pos_pe"], 1)
                nc.vector.tensor_scalar(pos1, psv(7, NT, NE), 1.0, None, ALU.add).then_inc(M["posd"], 1)
                dve.drain()
                nc.vector.tensor_tensor(rep, pos1, mask, ALU.mult)
                dve.drain()
                nc.vector.tensor_scalar(posm[:, 0:NE, :].rearrange("p e t -> p t e"), rep, 1.0, None, ALU.subtract)
                dve.wait_ge(M["cnt_pe"], 1)
                cnt = bank[7][0:NE, 0:P]
                nc.vector.tensor_scalar(novT[0:NE, :], cnt, float(CAP), None, ALU.is_gt)
                for n in range(2 * CAP, S, CAP):
                    dve.drain()
                    nc.vector.tensor_scalar(big[0:NE, 0:P], cnt, float(n), None, ALU.is_gt)
                    dve.drain()
                    nc.vector.tensor_tensor(novT[0:NE, :], novT[0:NE, :], big[0:NE, 0:P], ALU.add)
                dve.drain()
                dve.sem_inc(M["nov"], 1)
                dve.wait_ge(M["ov_pe"], 1)
                nc.vector.tensor_copy(ovs, bank[7][:, 128:128 + NE])
                nc.vector.tensor_copy(nov, bank[7][:, 256:256 + NE])
                dve.drain()
                nc.vector.tensor_tensor(oven, ovs, nov, ALU.add)
                dve.drain()
                nc.vector.tensor_copy(ntot, oven[:, NE - 1:NE])
                nc.vector.tensor_tensor(jcmp, oven.unsqueeze(1).to_broadcast([P, NOV, NE]),
                                        C["tile"].unsqueeze(2).to_broadcast([P, NOV, NE]), ALU.is_le)
                dve.drain()
                nc.vector.tensor_reduce(rank2, jcmp, axis=AX_X, op=ALU.add)
                dve.drain()
                nc.vector.tensor_scalar(etab, rank2, float(NE - 1), None, ALU.min)
                nc.vector.tensor_tensor(jcmp, jcmp, nov.unsqueeze(1).to_broadcast([P, NOV, NE]), ALU.mult)
                dve.drain()
                nc.vector.tensor_reduce(rank2, jcmp, axis=AX_X, op=ALU.add)
                dve.drain()
                nc.vector.tensor_tensor(rank2, C["tile"], rank2, ALU.subtract)
                dve.drain()
                nc.vector.tensor_scalar(q128, rank2, 1.0, float(CAP), ALU.add, ALU.mult)
                for t in range(NT):
                    dve.wait_ge(M["silu"], t + 1)
                    nc.vector.tensor_tensor(shid[:, t, 0:EH], shid[:, t, 256:512], bank[t][:, EH:2 * EH], ALU.mult).then_inc(M["hid"], 1)
                for t in range(NT):
                    dve.wait_ge(M["dn_done"], t + 1)
                    for i in range(2):
                        hh = h[:, t, i * 512:(i + 1) * 512]
                        nc.vector.tensor_tensor(hh, hh, bank[5 + i if t % 2 == 0 else i][:, :], ALU.add).then_inc(M["dn_out"], 1)

        if "h1" in dbg:
            dump(nc, sem("d4"), dbg["h1"], h[:, :, :])
        if "wts" in dbg:
            dump(nc, sem("d5"), dbg["wts"], tokw[:, 0:NE])
        front.close()
        F32R = mybir.dt.float32r
        back = ExitStack()
        ctx.enter_context(back)
        w_hl = back.enter_context(nc.sbuf_tensor("sb_w_hl", [P, 2, 2, 4096], F32R))
        xgT_hl = back.enter_context(nc.sbuf_tensor("sb_xgT_hl", [P, 2, KD, CAP], F32R))
        osb_t = back.enter_context(nc.sbuf_tensor("sb_rows_out", [P, 2, D], F32))
        osb = [osb_t[:, b, :] for b in range(2)]
        xg_f = [sem(f"s_xg{b}") for b in range(2)]
        stored = [sem(f"s_stored{b}") for b in range(2)]
        row_free = sem("s_row_free")
        dn = "oh list idx xt_pe xt_hi xt_lo hi lo gu silu hid hT_pe hT dn o_dve o_act".split()
        E = {n: sem("e_" + n) for n in dn}
        BL, BX, BH, BT2, BO = 0, (1, 2), 3, 4, (5, 6)
        wgp = gateT[:, 0:2 * KD, :].rearrange("p (k i) n -> p k (i n)", k=KD)
        wpl = work[:, 5104:7152].rearrange("p (c n) -> p c n", c=2)
        s_tail, s_xz, s_tick2, s_tick3 = sem("s_tail"), sem("s_xz"), sem("s_tick2"), sem("s_tick3")

        def load_down(sp, e, b):
            w = a["w_down"][0].rearrange("e (p c) n -> e p c n", c=2)
            sp.dma_start(Wd[b], w[e]).then_inc(s_wd[b], 16)

        def run(eng, step):
            step(0, 0, 0, first=True)
            with eng.Fori(0, NE // 2 - 1) as it:
                step(it * 2 + 1, 1, it)
                step(it * 2 + 2, 0, it + 1)
            step(NE - 1, 1, NE // 2 - 1, final=True)

        def list_products(pe, e, s):
            for t in range(NT):
                last = nc.tensor.matmul(bank[BL][:, 0:3], onehot[:, t, :], tokw[:, e, t, :], start=t == 0, stop=t == NT - 1)
            last.then_inc(s["list"], 1)

        def gathered_transposes(pe, half, src, s):
            rows = src.rearrange("q (p k) -> q k p", k=KD)
            for k in range(4 * half, 4 * half + 4):
                last = nc.tensor.transpose(bank[BX[half]][:, (k % 4) * P:(k % 4 + 1) * P], rows[:, k, :], ident)
            last.then_inc(s["xt_pe"], 1)

        def split_up_products(pe, b):
            w = w_hl[:, b].rearrange("p z (i k n) -> p z i k n", i=2, k=KD)
            n = 0
            for k in range(KD):
                for zx, zw in ((0, 0), (0, 1), (1, 0)):
                    last = nc.tensor.matmul(bank[BH][:, :], xgT_hl[:, zx, k, :], w[:, zw, :, k, :], start=n == 0, stop=n == 3 * KD - 1)
                    n += 1
            last.then_inc(E["gu"], 1)

        def hidden_transposes(pe, s):
            rows = hid.rearrange("q (p c) -> q c p", c=2)
            for c in range(2):
                last = nc.tensor.transpose(bank[BT2][:, c * P:(c + 1) * P], rows[:, c, :], ident)
            last.then_inc(s["hT_pe"], 1)

        def down_products(pe, wd, s):
            for i in range(2):
                for c in range(2):
                    last = nc.tensor.matmul(bank[BO[i]][:, :], hT[:, c, :], wd[:, c, i * 512:(i + 1) * 512],
                                            start=c == 0, stop=c == 1)
            last.then_inc(s["dn"], 1)

        with nc.Block() as block:
            @block.sync
            def _(sp):
                def next_gate_up(e, b):
                    for i in range(2):
                        sp.wait_ge(E["lo"], 2 * e + i - 3)
                        sp.sem_inc(s_tick3, 1)
                        load_gu(sp, e, b, i)

                def next_down(e, b):
                    sp.wait_ge(E["dn"], e - 1)
                    sp.sem_inc(s_tick3, 1)
                    load_down(sp, e, b)

                for i in range(2):
                    load_gu(sp, 1, 1, i)
                load_down(sp, 0, 0)
                load_down(sp, 1, 1)
                next_gate_up(2, 0)
                next_gate_up(3, 1)
                sp.dma_start(wgp, chunks(a["w_ple_gate"][0])).then_inc(s_tail, 16)
                with sp.Fori(1, NE // 2 - 1) as it:
                    for b in range(2):
                        next_gate_up(it * 2 + b + 2, b)
                        next_down(it * 2 + b, b)
                next_down(NE - 2, 0)
                next_down(NE - 1, 1)

            @block.gpsimd
            def _(pool):
                def gather(b):
                    pool.indirect_dma_start(out=xg[b], out_offset=None, in_=xn2_d,
                                            in_offset=bass.IndirectOffsetOnAxis(ap=idx[:, b:b + 1], axis=0),
                                            bounds_check=S - 1, oob_is_err=False).then_inc(xg_f[b], 16)

                def scatter(e, b, it):
                    pool.wait_ge(E["o_dve"], e + 2)
                    pool.wait_ge(E["o_act"], e + 2)
                    pool.sem_inc(s_tick2, 1)
                    pool.indirect_dma_start(out=rows_d, out_offset=bass.IndirectOffsetOnAxis(ap=didx[:, b:b + 1], axis=0),
                                            in_=osb[b], in_offset=None, bounds_check=8 * S - 1, oob_is_err=False).then_inc(stored[b], 16)
                    pool.wait_ge(stored[b], 16 * it + 16)
                    pool.sem_inc(row_free, 1)

                for b in range(2):
                    pool.sem_inc(row_free, 1)
                    nc.gpsimd.memset(xg[b], 0.0).then_inc(s_xz, 1)
                pool.wait_ge(s_xz, 2)
                for b in range(2):
                    pool.wait_ge(E["idx"], b + 1)
                    gather(b)

                def step(e, b, it, first=False, final=False):
                    if not final:
                        pool.wait_ge(E["idx"], e + 3)
                        pool.sem_inc(s_tick2, 1)
                        gather(b)
                    if not first:
                        scatter(e - 1, 1 - b, it if b else it - 1)
                run(pool, step)
                scatter(NE - 1, 1, NE // 2 - 1)
                pool.wait_ge(xg_f[0], 16 * (NE // 2 + 1))

            @block.tensor
            def _(pe):
                def move_rows(n_gathered, b):
                    pe.wait_ge(xg_f[b], n_gathered)
                    gathered_transposes(pe, 0, xg[b], E)
                    gathered_transposes(pe, 1, xg[b], E)

                def down(e, b, it):
                    pe.wait_ge(E["hT"], e + 1)
                    pe.wait_ge(s_wd[b], 16 * it + 16)
                    pe.wait_ge(E["o_dve"], e + 1)
                    pe.wait_ge(E["o_act"], e + 1)
                    down_products(pe, Wd[b], E)

                for b in range(2):
                    pe.wait_ge(E["oh"], b + 1)
                    list_products(pe, b, E)
                move_rows(16, 0)

                def step(e, b, it, first=False, final=False):
                    pe.wait_ge(E["xt_lo"], 2 * e + 2)
                    pe.wait_ge(E["lo"], 2 * e + 2)
                    split_up_products(pe, b)
                    if not final:
                        move_rows(16 * it + 16 + 16 * b, 1 - b)
                        pe.wait_ge(E["oh"], e + 3)
                        list_products(pe, e + 2, E)
                    if not first:
                        down(e - 1, 1 - b, it if b else it - 1)
                    pe.wait_ge(E["hid"], e + 1)
                    hidden_transposes(pe, E)
                run(pe, step)
                down(NE - 1, 1, NE // 2 - 1)

            @block.vector
            def _(dve):
                def one_hot(e):
                    nc.vector.tensor_tensor(onehot, C["slot"].unsqueeze(1).to_broadcast([P, NT, CAP]),
                                            posm[:, e, :].unsqueeze(2).to_broadcast([P, NT, CAP]), ALU.is_equal).then_inc(E["oh"], 1)

                def take_list(e, b):
                    dve.wait_ge(E["list"], e + 1)
                    nc.vector.tensor_scalar(idx[:, b:b + 1], bank[BL][:, 0:1], float(S), None, ALU.add).then_inc(E["idx"], 1)
                    nc.vector.tensor_copy(wts[:, bass.ds(e, 1)], bank[BL][:, 1:2])
                    nc.vector.tensor_scalar(dstf[:, bass.ds(e, 1)], bank[BL][:, 2:3], float(8 * S), None, ALU.add)

                def rest_of_weights(e, b):
                    for i in range(2):
                        dve.wait_ge(E["hi"], 2 * e + i + 1)
                        cols = slice(2048 * i, 2048 * i + 2048)
                        nc.vector.tensor_tensor(w_hl[:, b, 1, cols], raw[b][:, i, :], w_hl[:, b, 0, cols].bitcast(F32),
                                                ALU.subtract).then_inc(E["lo"], 1)

                def rest_of_rows(e):
                    for half in range(2):
                        dve.wait_ge(E["xt_hi"], 2 * e + half + 1)
                        ks = slice(4 * half, 4 * half + 4)
                        nc.vector.tensor_tensor(xgT_hl[:, 1, ks, :], psv(BX[half], 4, P), xgT_hl[:, 0, ks, :].bitcast(F32),
                                                ALU.subtract).then_inc(E["xt_lo"], 1)

                def rows_out(e, b):
                    dve.wait_ge(E["dn"], e + 1)
                    dve.wait_ge(row_free, e + 1)
                    nc.vector.tensor_copy(didx[:, b:b + 1], dstf[:, bass.ds(e, 1)])
                    nc.vector.tensor_scalar(osb[b][:, 0:512], bank[BO[0]][:, :], wts[:, bass.ds(e, 1)], None, ALU.mult).then_inc(E["o_dve"], 1)

                dve.sem_inc(E["o_dve"], 1)
                for b in range(2):
                    one_hot(b)
                    take_list(b, b)
                rest_of_weights(0, 0)
                rest_of_rows(0)

                def step(e, b, it, first=False, final=False):
                    if not final:
                        one_hot(e + 2)
                        rest_of_weights(e + 1, 1 - b)
                        rest_of_rows(e + 1)
                    dve.wait_ge(E["silu"], e + 1)
                    nc.vector.tensor_tensor(hid, sg, bank[BH][:, EH:2 * EH], ALU.mult).then_inc(E["hid"], 1)
                    if not final:
                        take_list(e + 2, b)
                    if not first:
                        rows_out(e - 1, 1 - b)
                run(dve, step)
                rows_out(NE - 1, 1)

            @block.scalar
            def _(act):
                def round_weights(e, b, it):
                    for i in range(2):
                        act.wait_ge(s_raw[b][i], 16 * it + 16)
                        nc.scalar.copy(w_hl[:, b, 0, 2048 * i:2048 * i + 2048], raw[b][:, i, :]).then_inc(E["hi"], 1)

                def round_rows(e):
                    for half in range(2):
                        act.wait_ge(E["xt_pe"], 2 * e + half + 1)
                        nc.scalar.copy(xgT_hl[:, 0, 4 * half:4 * half + 4, :], psv(BX[half], 4, P)).then_inc(E["xt_hi"], 1)

                def rows_out(e, b):
                    act.wait_ge(E["dn"], e + 1)
                    act.wait_ge(row_free, e + 1)
                    nc.scalar.activation(osb[b][:, 512:1024], bank[BO[1]][:, :], ACT.Copy, scale=wts[:, bass.ds(e, 1)]).then_inc(E["o_act"], 1)

                act.sem_inc(E["o_act"], 1)
                round_weights(0, 0, 0)
                round_rows(0)

                def step(e, b, it, first=False, final=False):
                    if not final:
                        if not first:
                            act.wait_ge(E["gu"], e)
                        round_weights(e + 1, 1 - b, it + 1 if b else it)
                    act.wait_ge(E["gu"], e + 1)
                    nc.scalar.activation(sg, bank[BH][:, 0:EH], ACT.Silu).then_inc(E["silu"], 1)
                    if not final:
                        round_rows(e + 1)
                    if not first:
                        rows_out(e - 1, 1 - b)
                    act.wait_ge(E["hT_pe"], e + 1)
                    nc.scalar.copy(hT, psv(BT2, 2, P)).then_inc(E["hT"], 1)
                run(act, step)
                rows_out(NE - 1, 1)

        V = {n: sem("v_" + n) for n in "oh list idx xg xt_pe xt_dve gate_up gu silu hid hT_pe hT down dn o_act stored".split()}
        slotq, w_v = sg[:, 0:CAP], sg[:, CAP:CAP + 1]
        xgT = osb_t[:, 1, :].rearrange("p (k n) -> p k n", k=KD)
        wgu = raw[0].rearrange("p i (k n) -> p i k n", k=KD)
        with nc.Block() as block:
            @block.sync
            def _(sp):
                more = sp.value_load(ntot[0:1, 0:1], min_val=0, max_val=NOV)
                with sp.If(more > 0):
                    with sp.Fori(0, more) as j:
                        e = sp.value_load(etab[0:1, bass.ds(j, 1)], min_val=0, max_val=NE - 1)
                        for i, n in enumerate(("w_gate", "w_up")):
                            sp.dma_start(raw[0][:, i, :], a[n][0].rearrange("e (p k) n -> e p (k n)", k=KD)[e]).then_inc(V["gate_up"], 16)
                        sp.dma_start(Wd[0], a["w_down"][0].rearrange("e (p c) n -> e p c n", c=2)[e]).then_inc(V["down"], 16)
                        sp.wait_ge(V["stored"], 16 * j + 16)
                        sp.sem_inc(s_tick3, 1)

            @block.gpsimd
            def _(pool):
                more = pool.value_load(ntot[0:1, 0:1], min_val=0, max_val=NOV)
                with pool.If(more > 0):
                    with pool.Fori(0, more) as j:
                        pool.wait_ge(V["idx"], j + 1)
                        pool.sem_inc(s_tick2, 1)
                        pool.indirect_dma_start(out=xg[0], out_offset=None, in_=xn2_d,
                                                in_offset=bass.IndirectOffsetOnAxis(ap=idx[:, 0:1], axis=0),
                                                bounds_check=S - 1, oob_is_err=False).then_inc(V["xg"], 16)
                        pool.wait_ge(V["o_act"], j + 1)
                        pool.sem_inc(s_tick2, 1)
                        pool.indirect_dma_start(out=rows_d, out_offset=bass.IndirectOffsetOnAxis(ap=didx[:, 0:1], axis=0),
                                                in_=osb[0], in_offset=None, bounds_check=8 * S - 1, oob_is_err=False).then_inc(V["stored"], 16)
                        pool.wait_ge(V["stored"], 16 * j + 16)

            @block.tensor
            def _(pe):
                more = pe.value_load(ntot[0:1, 0:1], min_val=0, max_val=NOV)
                with pe.If(more > 0):
                    with pe.Fori(0, more) as j:
                        e = pe.value_load(etab[0:1, bass.ds(j, 1)], min_val=0, max_val=NE - 1)
                        pe.wait_ge(V["oh"], j + 1)
                        list_products(pe, e, V)
                        pe.wait_ge(V["xg"], 16 * j + 16)
                        gathered_transposes(pe, 0, xg[0], V)
                        gathered_transposes(pe, 1, xg[0], V)
                        pe.wait_ge(V["xt_dve"], j + 1)
                        pe.wait_ge(V["gate_up"], 32 * j + 32)
                        for k in range(KD):
                            last = nc.tensor.matmul(bank[BH][:, :], xgT[:, k, :], wgu[:, :, k, :], start=k == 0, stop=k == KD - 1)
                        last.then_inc(V["gu"], 1)
                        pe.wait_ge(V["hid"], j + 1)
                        hidden_transposes(pe, V)
                        pe.wait_ge(V["hT"], j + 1)
                        pe.wait_ge(V["down"], 16 * j + 16)
                        down_products(pe, Wd[0], V)
                        pe.wait_ge(V["o_act"], j + 1)

            @block.vector
            def _(dve):
                more = dve.value_load(ntot[0:1, 0:1], min_val=0, max_val=NOV)
                with dve.If(more > 0):
                    with dve.Fori(0, more) as j:
                        e = dve.value_load(etab[0:1, bass.ds(j, 1)], min_val=0, max_val=NE - 1)
                        nc.vector.tensor_scalar(slotq, C["slot"], q128[:, bass.ds(j, 1)], None, ALU.add)
                        dve.drain()
                        nc.vector.tensor_tensor(onehot, slotq.unsqueeze(1).to_broadcast([P, NT, CAP]),
                                                posm[:, e, :].unsqueeze(2).to_broadcast([P, NT, CAP]), ALU.is_equal).then_inc(V["oh"], 1)
                        dve.wait_ge(V["list"], j + 1)
                        nc.vector.tensor_scalar(idx[:, 0:1], bank[BL][:, 0:1], float(S), None, ALU.add).then_inc(V["idx"], 1)
                        nc.vector.tensor_copy(w_v, bank[BL][:, 1:2])
                        nc.vector.tensor_scalar(didx[:, 0:1], bank[BL][:, 2:3], float(8 * S), None, ALU.add)
                        dve.wait_ge(V["xt_pe"], 2 * j + 2)
                        for half in range(2):
                            last = nc.vector.tensor_copy(xgT[:, 4 * half:4 * half + 4, :], psv(BX[half], 4, P))
                        last.then_inc(V["xt_dve"], 1)
                        dve.wait_ge(V["silu"], j + 1)
                        nc.vector.tensor_tensor(hid, hid, bank[BH][:, EH:2 * EH], ALU.mult).then_inc(V["hid"], 1)
                        dve.wait_ge(V["hT_pe"], j + 1)
                        nc.vector.tensor_copy(hT, psv(BT2, 2, P)).then_inc(V["hT"], 1)
                        dve.wait_ge(V["dn"], j + 1)
                        for half in range(2):
                            last = nc.vector.tensor_scalar(osb[0][:, 512 * half:512 * half + 512], bank[BO[half]][:, :], w_v, None, ALU.mult)
                        last.then_inc(V["o_act"], 1)
                        dve.wait_ge(V["stored"], 16 * j + 16)

            @block.scalar
            def _(act):
                more = act.value_load(ntot[0:1, 0:1], min_val=0, max_val=NOV)
                with act.If(more > 0):
                    with act.Fori(0, more) as j:
                        act.wait_ge(V["gu"], j + 1)
                        nc.scalar.activation(hid, bank[BH][:, 0:EH], ACT.Silu).then_inc(V["silu"], 1)
                        act.wait_ge(V["hid"], j + 1)

        back.close()
        xnT = sb("xn3T", [P, KD, 2 * P])
        r2 = sb("rows_even", [P, 8192])
        r3 = sb("rows_odd", [P, 8192])
        prow = r1[:, 0:1024].rearrange("p (t n) -> p t n", t=NT)
        pTt = r1[:, 1024:2048].rearrange("p (c n) -> p c n", c=2)
        gple, gfin = r1[:, 2048:3072], r1[:, 3072:4096]
        xn3, sigt = r1[:, 4096:5120], r1[:, 5120:6144]
        rows8 = [r2[:, 0:8192].rearrange("p (j n) -> p j n", j=8), r3[:, 0:8192].rearrange("p (j n) -> p j n", j=8)]
        xn3T = xnT[:, :, :].rearrange("p k (b n) -> p b k n", b=2)
        tn = "p_tp p_tc emb_pe emb ms rr xn xt_pe xt gate_pe sig gated ms2 rr2 out".split()
        T = {n: sem("t_" + n) for n in tn}
        s_rows = [sem(f"t_rows{t}") for t in range(NT)]
        s_p, s_gp, s_wpl, s_out = sem("s_p"), sem("s_gp"), sem("s_wpl"), sem("s_out")
        part = small[:, 96:112]
        with nc.Block() as block:
            @block.sync
            def _(sp):
                sp.dma_start(prow, a["p"][0, 0].rearrange("(t p) n -> p t n", p=P)).then_inc(s_p, 16)
                sp.dma_start(wpl, a["w_ple"][0].rearrange("(c p) n -> p c n", p=P)).then_inc(s_wpl, 16)
                sp.dma_start(gple, a["g_ple"][0].partition_broadcast(P)).then_inc(s_gp, 16)
                sp.dma_start(gfin, a["g_final"].partition_broadcast(P)).then_inc(s_gp, 16)
                for t in range(NT):
                    if t >= 2:
                        sp.wait_ge(T["ms"], t - 1)
                    sp.dma_start(rows8[t % 2], rows_d[t * 8 * P:(t + 1) * 8 * P, :].rearrange("(p j) n -> p j n", j=8)).then_inc(s_rows[t], 16)
                for t in range(NT):
                    sp.wait_ge(T["out"], t + 1)
                    sp.dma_start(a["out"][0, t * P:(t + 1) * P, :], h[:, t, :]).then_inc(s_out, 16)
                sp.wait_ge(s_out, 16 * NT)

            @block.gpsimd
            def _(pool):
                for t in range(NT):
                    for n, (m, r) in enumerate((("ms", "rr"), ("ms2", "rr2"))):
                        if n == 1 and t == 0:
                            continue
                        tt = t - n
                        pool.wait_ge(T[m], tt + 1)
                        nc.gpsimd.tensor_tensor(part[:, 8 * n + 4 + tt:8 * n + 5 + tt], part[:, 8 * n + tt:8 * n + tt + 1],
                                                C["nhalf"][:, 0:1], ALU.pow).then_inc(T[r], 1)
                pool.wait_ge(T["ms2"], NT)
                nc.gpsimd.tensor_tensor(part[:, 15:16], part[:, 11:12], C["nhalf"][:, 0:1], ALU.pow).then_inc(T["rr2"], 1)

            @block.tensor
            def _(pe):
                pe.wait_ge(s_p, 16)
                for c in range(2):
                    for t in range(NT):
                        last = nc.tensor.transpose(bank[c][:, t * P:(t + 1) * P], prow[:, t, c * P:(c + 1) * P], ident)
                    last.then_inc(T["p_tp"], 1)
                pe.wait_ge(T["p_tc"], 2)
                pe.wait_ge(s_wpl, 16)
                for t in range(NT):
                    if t >= 2:
                        pe.wait_ge(T["emb"], 2 * (t - 1))
                    for i in range(2):
                        for c in range(2):
                            last = nc.tensor.matmul(bank[2 + 2 * (t % 2) + i][:, :], pTt[:, c, t * P:(t + 1) * P],
                                                    wpl[:, c, i * 512:(i + 1) * 512], start=c == 0, stop=c == 1)
                        last.then_inc(T["emb_pe"], 1)
                pe.wait_ge(s_tail, 16)
                for t in range(NT):
                    pe.wait_ge(T["xn"], t + 1)
                    for k in range(KD):
                        last = nc.tensor.transpose(bank[k // 4][:, (k % 4) * P:(k % 4 + 1) * P], xn3[:, k * P:(k + 1) * P], ident)
                    last.then_inc(T["xt_pe"], 1)
                    pe.wait_ge(T["xt"], 2 * t + 2)
                    if t == 0:
                        pe.wait_ge(T["emb"], 8)
                    for i in range(2):
                        for k in range(KD):
                            last = nc.tensor.matmul(bank[2 + 2 * (t % 2) + i][:, :], xn3T[:, t % 2, k, :],
                                                    wgp[:, k, i * 512:(i + 1) * 512], start=k == 0, stop=k == KD - 1)
                        last.then_inc(T["gate_pe"], 1)

            @block.scalar
            def _(act):
                for c in range(2):
                    act.wait_ge(T["p_tp"], c + 1)
                    nc.scalar.copy(pTt[:, c, :], bank[c][:, :]).then_inc(T["p_tc"], 1)
                for t in range(NT):
                    for i in range(2):
                        act.wait_ge(T["emb_pe"], 2 * t + i + 1)
                        nc.scalar.copy(y[:, t, i * 512:(i + 1) * 512], bank[2 + 2 * (t % 2) + i][:, :]).then_inc(T["emb"], 1)
                for t in range(NT):
                    act.wait_ge(T["xt_pe"], t + 1)
                    for i in range(2):
                        nc.scalar.copy(xn3T[:, t % 2, 4 * i:4 * i + 4, :], psv(i, 4, P)).then_inc(T["xt"], 1)
                    if t:
                        act.wait_ge(T["gated"], 2 * t)
                    for i in range(2):
                        act.wait_ge(T["gate_pe"], 2 * t + i + 1)
                        nc.scalar.activation(sigt[:, i * 512:(i + 1) * 512], bank[2 + 2 * (t % 2) + i][:, :], ACT.Sigmoid).then_inc(T["sig"], 1)

            @block.vector
            def _(dve):
                def finish(t):
                    for i in range(2):
                        cols = slice(i * 512, (i + 1) * 512)
                        dve.wait_ge(T["sig"], 2 * t + i + 1)
                        nc.vector.tensor_tensor(y[:, t, cols], y[:, t, cols], sigt[:, cols], ALU.mult).then_inc(T["gated"], 1)
                    dve.drain()
                    nc.vector.tensor_tensor(h[:, t, :], h[:, t, :], y[:, t, :], ALU.add)
                    dve.drain()
                    norm_sums(dve, t, h[:, t, :], y[:, t, :], part[:, 8:12]).then_inc(T["ms2"], 1)
                    dve.wait_ge(T["rr2"], t + 1)
                    nc.vector.scalar_tensor_tensor(out=h[:, t, :], in0=h[:, t, :], scalar=part[:, 12 + t:13 + t], in1=gfin,
                                                   op0=ALU.mult, op1=ALU.mult).then_inc(T["out"], 1)

                dve.wait_ge(s_gp, 32)
                dve.wait_ge(T["emb"], 8)
                for t in range(NT):
                    r = rows8[t % 2]
                    dve.wait_ge(s_rows[t], 16)
                    for n in (4, 2, 1):
                        nc.vector.tensor_tensor(r[:, 0:n, :], r[:, 0:n, :], r[:, n:2 * n, :], ALU.add)
                        dve.drain()
                    nc.vector.tensor_tensor(h[:, t, :], h[:, t, :], r[:, 0, :], ALU.add)
                    dve.drain()
                    norm_sums(dve, t, h[:, t, :], r[:, 1, :], part).then_inc(T["ms"], 1)
                    if t:
                        dve.wait_ge(T["xt_pe"], t)
                    dve.wait_ge(T["rr"], t + 1)
                    nc.vector.scalar_tensor_tensor(out=xn3, in0=h[:, t, :], scalar=part[:, 4 + t:5 + t], in1=gple,
                                                   op0=ALU.mult, op1=ALU.mult).then_inc(T["xn"], 1)
                    if t:
                        finish(t - 1)
                finish(NT - 1)


def load_b_group(sp, w_in, wBk, wBq, wBv, g, s):
    for i, col in enumerate((COL_KS, COL_KW, COL_KCR, COL_VCR)):
        for two in range(2):
            sp.dma_start(wBk[:, i, :, two, :], w_in[:, :, bass.ds(g * DH + col, DH)]).then_inc(s, 16)
    for i, col in enumerate((COL_VS, COL_VW)):
        sp.dma_start(wBv[:, :, i, :], w_in[:, :, bass.ds(g * DH + col, DH)]).then_inc(s, 16)
    sp.dma_start(wBq, w_in[:, :, bass.ds(g * 4 * DH + COL_QB, 4 * DH)]).then_inc(s, 16)


def dump(nc, s, dst, src):
    with nc.Block() as block:
        @block.sync
        def _(sp):
            sp.dma_start(dst, src).then_inc(s, 16)
            sp.wait_ge(s, 16)


_INS = ["x", "p", "g_mix", "w_in", "cmp_pos_k", "cmp_w1_k", "cmp_b1_k", "cmp_w2_k", "cmp_pos_v", "cmp_w1_v", "cmp_b1_v",
        "cmp_w2_v", "w_branch_a", "w_branch_b", "w_out", "g_ffn", "w_router", "router_bias", "w_gate", "w_up", "w_down",
        "ws_gate", "ws_up", "ws_down", "g_ple", "w_ple_gate", "w_ple", "g_final"]


def kernel(**inputs):
    import concourse.bacc as bacc
    from concourse.bass_utils import run_bass_kernel_spmd

    nc = bacc.Bacc("TRN2", target_bir_lowering=False, num_devices=1)
    arrays = {"in_" + n: np.ascontiguousarray(inputs[n]) for n in _INS}
    arrays["in_cst"] = constants()[0]
    a = {n[3:]: nc.dram_tensor(n, v.shape, mybir.dt.from_np(v.dtype), kind="ExternalInput").ap() for n, v in arrays.items()}
    a["out"] = nc.dram_tensor("out_0", (1, S, D), F32, kind="ExternalOutput").ap()
    build(nc, a)
    r = run_bass_kernel_spmd(nc, [arrays], core_ids=[0])
    return r.results[0]["out_0"]
```

```python
from contextlib import ExitStack

import numpy as np

import concourse.bass as bass
from concourse import mybir

F32 = mybir.dt.float32
F32R = mybir.dt.float32r
I32 = mybir.dt.int32
BF16 = mybir.dt.bfloat16
ALU = mybir.AluOpType
ACT = mybir.ActivationFunctionType
AX_X = mybir.AxisListType.X

P = 128
S = 512
D = 1024
NT = S // P
KD = D // P
DH = 64
NH = 8
PLE = 256
EPS = 1e-6
BIG = 1e30
WIDTH_A = NH * DH
COL_QA, COL_KA, COL_VA, COL_QB = 0, WIDTH_A, 2 * WIDTH_A, 3 * WIDTH_A
COL_KCR = 4 * WIDTH_A
COL_VCR, COL_KS, COL_VS, COL_KW, COL_VW, COL_GN = (COL_KCR + 128 * i for i in range(1, 7))
COL_GA = COL_GN + 3 * NH
COL_GB = COL_GA + D
CMP_STRIDE, CMP_BLOCK = 16, 32
NC = S // CMP_STRIDE - 1
NE = 64
NG = 8
EH = 256
CAP = 128
MOVES = (48, 64, 80, 96, CAP)
ROUTED_SCALE = 2.5
NOV = (S * 8 - NE) // CAP
WORK = 6631
PASSES = ((0, 0), (0, 1), (1, 0))
NPAD = 2


def constants():
    p = np.arange(P)[:, None].astype(np.float64)
    c = np.arange(S)[None, :]
    dist = p + (S - P) - c
    count = ((dist >= 0) & (dist <= 128)).astype(int) + ((dist >= 0) & (dist % 4 == 0)) + ((dist >= 0) & (dist % 16 == 0))
    mdil = np.where(count > 0, -np.log(np.maximum(count, 1)), BIG)
    mfull = np.where(dist >= 0, 0.0, BIG)
    tok = (np.arange(NT)[None, :, None] * P + p[:, :, None])
    dcmp = tok - (np.arange(NC)[None, None, :] * CMP_STRIDE + CMP_BLOCK - 1)
    mcmp = np.where(dcmp >= 0, 0.0, BIG)
    slopes = 2.0 ** (-8.0 * np.arange(1, 2 * NH + 1) / (2 * NH))
    row = lambda v: np.broadcast_to(np.asarray(v, np.float64).reshape(1, -1), (P, np.asarray(v).size))
    e = np.arange(NE)
    tri64 = np.zeros((P, NE))
    tri64[:NE] = e[:, None] < e[None, :]
    g = np.arange(NG)
    parts = [
        ("ident", np.eye(P)),
        ("slot", row(np.arange(CAP))),
        ("tri", p < np.arange(P)[None, :]),
        ("ones", np.ones((P, P))),
        ("dist", dist),
        ("mdil", mdil),
        ("mfull", mfull),
        ("dcmp", dcmp.reshape(P, -1)),
        ("mcmp", mcmp.reshape(P, -1)),
        ("slopes_a", row(slopes[0::2])),
        ("slopes_b", row(slopes[1::2])),
        ("tok_a", p - P + 0 * np.arange(NT)[None, :]),
        ("tok_b", 0 * p + P * (np.arange(NT)[None, :] - (NT - 1))),
        ("tri64", tri64),
        ("before8", row((g[:, None] > g[None, :]).astype(float))),
        ("tile", row(np.arange(NOV))),
        ("nhalf", row([-0.5] * NT)),
    ]
    place, at = {}, 0
    for name, a in parts:
        place[name] = (at, a.shape[1])
        at += a.shape[1]
    return np.ascontiguousarray(np.concatenate([a for _, a in parts], axis=1).astype(np.float32)), place


def build(nc, a, dbg=None):
    dbg = dbg or {}
    place = constants()[1]
    ncst = sum(n for _, n in place.values())
    xn2_d = nc.dram_tensor("xn2_rows", (S, D), F32, kind="Internal").ap()
    rows_d = nc.dram_tensor("expert_rows", (S * 8, D), F32, kind="Internal").ap()

    ctx = ExitStack()
    with ctx:
        def sb(name, shape, dt=F32):
            return ctx.enter_context(nc.sbuf_tensor("sb_" + name, shape, dt))

        def ps(name, shape, dt=F32):
            return ctx.enter_context(nc.psum_tensor(name, shape, dt))

        def sem(name):
            return ctx.enter_context(nc.semaphore(name))

        cst = sb("cst", [P, ncst])
        C = {k: cst[:, o:o + n] for k, (o, n) in place.items()}
        ident = C["ident"]
        h = sb("h", [P, NT, D])
        y = sb("y", [P, NT, D])
        gateT = sb("gateT", [P, 2 * KD, S])
        r1 = sb("r1", [P, 6144])
        work = sb("work", [P, WORK])
        small = sb("small", [P, 640])
        front = ExitStack()
        ctx.enter_context(front)
        x_hl = front.enter_context(nc.sbuf_tensor("sb_x_hl", [P, 2, KD, S], F32R))
        w_hl = front.enter_context(nc.sbuf_tensor("sb_w6_hl", [P, 6, 2, KD, P], F32R))
        gn_hl = front.enter_context(nc.sbuf_tensor("sb_gn_hl", [P, 2, KD, 24], F32R))
        bank = [ps(f"bank{i}", [P, 512]) for i in range(8)]

        def psv(i, *shape):
            n = int(np.prod(shape))
            v = bank[i][:, 0:n]
            if len(shape) == 2:
                return v.rearrange("p (a b) -> p a b", a=shape[0])
            return v

        def chunks(ap):
            return ap.rearrange("(k p) n -> p k n", p=P)

        w_in = chunks(a["w_in"][0])

        raw_at = [r1[:, 1024 * i:1024 * (i + 1)].rearrange("p (k n) -> p k n", k=KD) for i in range(5)]
        s_rawp = [sem(f"s_rawp{i}") for i in range(5)]
        s_split = sem("s_split")
        s_w_hi = sem("s_w_hi")
        A_PIECE = lambda it, j: it * 5 + j
        KV_PIECE, B_PIECE = 20, lambda it, j: it * 3 + 26 + j
        WM_PIECE, WO_PIECE = 38, 46
        SLOT_KV = [5, 0, 1, 2, 3, 4]
        SLOT_WM = [0, 1, 2, 5, 3, 4, 0, 1]
        WO = [(0, 2), (3, 5), (1, 3), (2, 4), (4, 0), (5, 1), (6, 2), (7, 3)]
        SLOT_OF = SLOT_WM + [slot for _, slot in WO]
        buf_of = [n % 5 for n in range(29)] + [4, 0, 1] * 3 + [(n - 36) % 5 for n in range(38, 54)]
        landed, before, so_far, last_use = [], [], [0] * 5, [0] * 5
        for n, b_ in enumerate(buf_of):
            so_far[b_] += 32 if n in [B_PIECE(it, 0) for it in range(4)] or WM_PIECE <= n < WO_PIECE else 16
            landed.append(so_far[b_])
            before.append(last_use[b_])
            last_use[b_] = n + 1

        def load_piece(sp, n, cols):
            if before[n]:
                sp.wait_ge(s_split, before[n])
            sp.dma_start(raw_at[buf_of[n]], cols).then_inc(s_rawp[buf_of[n]], 16)

        def split_piece(pool, buf, slot):
            nc.gpsimd.tensor_copy(w_hl[:, slot, 0], raw_at[buf])
            pool.drain()
            rest_of_piece(buf, slot)

        def rest_of_piece(buf, slot):
            nc.gpsimd.tensor_tensor(w_hl[:, slot, 1], raw_at[buf], w_hl[:, slot, 0].bitcast(F32), ALU.subtract).then_inc(s_split, 1)

        def wide_product(out, slot):
            n = 0
            for k in range(KD):
                for zx, zw in PASSES:
                    last = nc.tensor.matmul(out, w_hl[:, slot, zw, k, :], x_hl[:, zx, k, :], start=n == 0, stop=n == 3 * KD - 1)
                    n += 1
            return last

        s_cst, s_ident, s_x, s_g = sem("s_cst"), sem("s_ident"), [sem(f"s_x{t}") for t in range(NT)], sem("s_g")

        w2 = r1[:, 5120:5504].rearrange("p (c n) -> p c n", c=2)
        b1c = small[:, 104:108]
        pos_rows = r1[0:32, 5504:5632]
        pos2, pos2x = small[:, 108:140], small[:, 448:480]
        gn_w = work[:, 5880:6072].rearrange("p (k n) -> p k n", k=KD)
        s_gn, s_w2, s_pos = sem("s_gn"), sem("s_w2"), sem("s_pos")
        gates = small[:, 0:96].rearrange("p (t n) -> p t n", t=NT)
        gbc = work[:, 0:D]
        ms, rr = small[:, 96:100], small[:, 100:104]

        def norm_sums(dve, t, src, junk, msum):
            return nc.vector.tensor_tensor_reduce(out=junk, in0=src, in1=src, scale=1.0 / D, scalar=EPS,
                                                  op0=ALU.mult, op1=ALU.add, accum_out=msum[:, t:t + 1])

        def round_first(act, j):
            act.wait_ge(s_rawp[j], 16)
            nc.scalar.copy(w_hl[:, j, 0], raw_at[j]).then_inc(s_w_hi, 1)

        s_ms, s_rr, s_xn, s_tp, s_hi, s_lo = map(sem, "s_ms s_rr s_xn s_tp s_x_hi s_x_lo".split())
        with nc.Block() as block:
            @block.sync
            def _(sp):
                for t in range(NT):
                    sp.dma_start(h[:, t, :], a["x"][0, t * P:(t + 1) * P, :]).then_inc(s_x[t], 16)
                    if t == 0:
                        sp.dma_start(cst[:, 0:P], a["cst"][:, 0:P]).then_inc(s_ident, 16)
                        o = place["nhalf"][0]
                        sp.dma_start(cst[:, o:o + NT], a["cst"][:, o:o + NT]).then_inc(s_ident, 16)
                for j, col in enumerate((COL_QA, COL_KA, COL_VA, COL_GA, COL_GA + P)):
                    load_piece(sp, A_PIECE(0, j), w_in[:, :, col:col + P])
                    if j == 1:
                        sp.dma_start(cst[:, P:o], a["cst"][:, P:o]).then_inc(s_cst, 16)
                sp.dma_start(gn_w, w_in[:, :, COL_GN:COL_GN + 24]).then_inc(s_gn, 16)
                sp.dma_start(w2[:, :, 0:DH], a["cmp_w2_k"][0].rearrange("(c p) n -> p c n", p=P)).then_inc(s_w2, 16)
                sp.dma_start(w2[:, :, DH:2 * DH], a["cmp_w2_k"][0].rearrange("(c p) n -> p c n", p=P)).then_inc(s_w2, 16)
                sp.dma_start(w2[:, :, 2 * DH:3 * DH], a["cmp_w2_v"][0].rearrange("(c p) n -> p c n", p=P)).then_inc(s_w2, 16)
                for i, n in enumerate("kv"):
                    sp.dma_start(b1c[:, 2 * i:2 * i + 2], a["cmp_b1_" + n][0].rearrange("(c p) -> p c", p=P),
                                 allow_slow_non_contiguous=True).then_inc(s_w2, 16)
                    sp.dma_start(pos_rows[16 * i:16 * i + 16, :],
                                 a["cmp_pos_" + n][0].rearrange("(t two) d -> t (two d)", two=2)).then_inc(s_pos, 16)

            @block.gpsimd
            def _(pool):
                pool.dma_start(gbc, a["g_mix"][0].partition_broadcast(P)).then_inc(s_g, 16)
                pool.wait_ge(s_ident, 32)
                for t in range(NT):
                    pool.wait_ge(s_ms, t + 1)
                    nc.gpsimd.tensor_tensor(rr[:, t:t + 1], ms[:, t:t + 1], C["nhalf"][:, 0:1], ALU.pow).then_inc(s_rr, 1)
                for j in range(2):
                    pool.wait_ge(s_w_hi, j + 1)
                    rest_of_piece(j, j)

            @block.vector
            def _(dve):
                for t in range(NT):
                    dve.wait_ge(s_x[t], 16)
                    norm_sums(dve, t, h[:, t, :], y[:, t, :], ms).then_inc(s_ms, 1)
                    if t:
                        if t == 1:
                            dve.wait_ge(s_g, 16)
                        dve.wait_ge(s_rr, t)
                        nc.vector.scalar_tensor_tensor(out=y[:, t - 1, :], in0=h[:, t - 1, :], scalar=rr[:, t - 1:t], in1=gbc,
                                                       op0=ALU.mult, op1=ALU.mult).then_inc(s_xn, 1)
                dve.wait_ge(s_rr, NT)
                nc.vector.scalar_tensor_tensor(out=y[:, NT - 1, :], in0=h[:, NT - 1, :], scalar=rr[:, NT - 1:NT], in1=gbc,
                                               op0=ALU.mult, op1=ALU.mult).then_inc(s_xn, 1)
                for k in range(KD):
                    dve.wait_ge(s_hi, k + 1)
                    nc.vector.tensor_tensor(x_hl[:, 1, k, :], bank[k][:, :], x_hl[:, 0, k, :].bitcast(F32), ALU.subtract).then_inc(s_lo, 1)

            @block.tensor
            def _(pe):
                pe.wait_ge(s_ident, 32)
                for t in range(NT):
                    pe.wait_ge(s_xn, t + 1)
                    for k in range(KD):
                        last = nc.tensor.transpose(bank[k][:, t * P:(t + 1) * P], y[:, t, k * P:(k + 1) * P], ident)
                        if t == NT - 1:
                            last.then_inc(s_tp, 1)

            @block.scalar
            def _(act):
                for j in range(2):
                    round_first(act, j)
                for k in range(KD):
                    act.wait_ge(s_tp, k + 1)
                    nc.scalar.copy(x_hl[:, 0, k, :], bank[k][:, :]).then_inc(s_hi, 1)

        w1 = [h[:, :, :].rearrange("p a b -> p (a b)").rearrange("p (t n) -> p t n", t=16),
              gateT[:, KD:2 * KD, :].rearrange("p a b -> p (a b)").rearrange("p (t n) -> p t n", t=16)]
        rowsum = small[:, 140:148]
        rsum3 = small[:, 148:154].rearrange("p (b i) -> p b i", b=2)
        coef = small[:, 436:444]
        minus_max = small[:, 158:160]
        slope2 = small[:, 160:162]
        gts = small[:, 164:188].rearrange("p (t b n) -> p t b n", t=NT, b=3)
        vc_sb = small[:, 480:608]
        kcT = small[:, 608:640]
        hTc = small[:, 188:436].rearrange("p (i c n) -> p i c n", i=2, c=2)

        qT = work[:, 0:512]
        kT = work[:, 512:1536].rearrange("p (i n) -> p i n", i=2)
        vvA = work[:, 1536:2048].rearrange("p (t n) -> p t n", t=NT)
        vvB = work[:, 1536:2560].rearrange("p (t n) -> p t n", t=NT)
        bias = work[:, 2560:3584].rearrange("p (i n) -> p i n", i=2)
        bias_c = work[:, 3584:3832].rearrange("p (i t n) -> p i t n", i=2, t=NT)
        sc = work[:, 3832:4856].rearrange("p (i n) -> p i n", i=2)
        pT = work[:, 4856:5880].rearrange("p (i n) -> p i n", i=2)
        gnT = sc[0:24, 0, :]

        names = "projected evicted scored biased exped transposed copied pv_done y_done f_done f_evicted"
        A = {n: sem("a_" + n) for n in (names + " vT v_rows").split()}
        B = {n: sem("b_" + n) for n in names.split()}
        s_tick = sem("s_tick")
        s_hid, s_gelu = sem("s_hid"), sem("s_gelu")
        ysum = r1[:, 5632:5888].rearrange("p (b i n) -> p b i n", b=2, i=2)
        s_w1, s_posT = sem("s_w1"), sem("s_posT")
        s_xagain = sem("s_xagain")
        s_hg = sem("s_head_gates")
        BS, BT, BV, BJ, BF = (0, 1), 2, (3, 4), (5, 6), 7

        unitsA = [dict(rows=64 * hh, qt=qt, n=P * (qt + 1), k=0, bias=("a", hh), v=hh, vv=vvA, group=hh * NT + qt, br=0)
                  for hh in range(2) for qt in range(NT)]
        unitsB = [dict(rows=64 * g, qt=qt, n=NC if br == 0 else P * (qt + 1), k=br - 1, bias=("c" if br == 0 else "a", g),
                       v=g if br == 0 else 2 * (br - 1) + g, vv=vvB, group=g * NT + qt, br=br)
                  for g in range(2) for qt in range(NT) for br in range(3)]
        fillA = {w: (2 * w, 2 * w + 2) for w in range(8)}
        fillB, n = {}, 0
        for w in range(24):
            if w % 3 != 0:
                fillB[w] = (n, n + 1)
                n += 1
        SLOT_GATE = 3

        def n_chunks(u):
            return 1 if u["n"] == NC else u["n"] // P

        def unit_products(pe, u, w, it, per, s):
            rows = slice(u["rows"], u["rows"] + 64)
            lhsT = qT[rows, u["qt"] * P:(u["qt"] + 1) * P]
            rhs = kcT[rows, 0:NC] if u["n"] == NC else kT[rows, u["k"], 0:u["n"]]
            nc.tensor.matmul(bank[BS[w % 2]][:, 0:u["n"]], lhsT, rhs, start=True, stop=True).then_inc(s["scored"], 1)

        def unit_transposes(pe, u, w, it, per, s):
            pe.wait_ge(s["exped"], it * per + w + 1)
            for j in range(n_chunks(u)):
                m = min(P, u["n"])
                last = nc.tensor.transpose(bank[BT][0:m, j * P:(j + 1) * P], sc[:, w % 2, j * P:j * P + m], ident)
            last.then_inc(s["transposed"], 1)

        def unit_values(pe, u, w, it, per, s, groups):
            pe.wait_ge(s["copied"], it * per + w + 1)
            if u["br"] == 0:
                pe.wait_ge(s["y_done"], it * groups + u["group"] + 1)
            out = bank[BV[u["group"] % 2]][:, u["br"] * DH:(u["br"] + 1) * DH]
            nch = n_chunks(u)
            for j in range(nch):
                m = min(P, u["n"])
                cols = slice(u["v"] * DH, (u["v"] + 1) * DH)
                rhs = vc_sb[0:NC, cols] if u["n"] == NC else u["vv"][:, j, cols]
                last = nc.tensor.matmul(out, pT[0:m, w % 2, j * P:(j + 1) * P], rhs, start=j == 0, stop=j == nch - 1)
            last.then_inc(s["pv_done"], 1)

        def filler(pe, lo, hi, it, s, first_piece):
            for m in range(lo, hi):
                c, k = divmod(m, KD)
                if k == 0:
                    pe.wait_ge(s_split, first_piece(it, c) + 1)
                    pe.wait_ge(s["f_evicted"], it * 2 + c + 1)
                for j, (zx, zw) in enumerate(PASSES):
                    last = nc.tensor.matmul(bank[BF][:, :], w_hl[:, SLOT_GATE + c, zw, k, :], x_hl[:, zx, k, :],
                                            start=k + j == 0, stop=k == KD - 1 and j == 2)
                if k == KD - 1:
                    last.then_inc(s["f_done"], 1)

        def attend_pe(pe, units, fill, it, s, first_piece):
            per = len(units)
            unit_products(pe, units[0], 0, it, per, s)
            for w, u in enumerate(units):
                if w + 1 < per:
                    unit_products(pe, units[w + 1], w + 1, it, per, s)
                if w in fill:
                    filler(pe, *fill[w], it, s, first_piece)
                if w:
                    unit_values(pe, units[w - 1], w - 1, it, per, s, 8)
                unit_transposes(pe, u, w, it, per, s)
            unit_values(pe, units[-1], per - 1, it, per, s, 8)

        def unit_bias(dve, u, w, it, per, s):
            dve.wait_ge(s["scored"], it * per + w + 1)
            dve.sem_inc(s_tick, 1)
            b = bias_c[:, u["bias"][1], u["qt"], :] if u["n"] == NC else bias[:, u["bias"][1], S - u["n"]:S]
            nc.vector.tensor_tensor_reduce(out=sc[:, w % 2, 0:u["n"]], in0=bank[BS[w % 2]][:, 0:u["n"]], in1=b,
                                           scale=1.0, scalar=0.1 * BIG, op0=ALU.add, op1=ALU.min,
                                           accum_out=minus_max[:, w % 2:w % 2 + 1]).then_inc(s["biased"], 1)

        def unit_exp(act, u, w, it, per, s, sums):
            act.wait_ge(s["biased"], it * per + w + 1)
            nc.scalar.activation(sc[:, w % 2, 0:u["n"]], sc[:, w % 2, 0:u["n"]], ACT.Exp, scale=-1.0,
                                 bias=minus_max[:, w % 2:w % 2 + 1], accum_out=sums).then_inc(s["exped"], 1)

        def unit_copy(act, u, w, it, per, s):
            act.wait_ge(s["transposed"], it * per + w + 1)
            m, n = min(P, u["n"]), P * n_chunks(u)
            nc.scalar.copy(pT[0:m, w % 2, 0:n], bank[BT][0:m, 0:n]).then_inc(s["copied"], 1)

        def attend_act(act, units, it, s, sums):
            per = len(units)
            for w, u in enumerate(units):
                unit_exp(act, u, w, it, per, s, sums(u, w))
                unit_copy(act, u, w, it, per, s)

        def attend_dve(dve, units, fill, it, s, put, gate_at):
            per = len(units)
            unit_bias(dve, units[0], 0, it, per, s)
            for w, u in enumerate(units):
                if w + 1 < per:
                    unit_bias(dve, units[w + 1], w + 1, it, per, s)
                if w in fill and fill[w][1] % KD == 0:
                    c = fill[w][1] // KD - 1
                    dve.wait_ge(s["f_done"], it * 2 + c + 1)
                    nc.vector.tensor_copy(gate_at(c), bank[BF][:, :]).then_inc(s["f_evicted"], 1)
                if w and units[w]["group"] != units[w - 1]["group"]:
                    put(dve, units[w - 1], w - 1)
            put(dve, units[-1], per - 1)

        def load_queries(sp, buf, i):
            for g in range(2):
                sp.dma_start(raw_at[buf][:, :, g * DH:(g + 1) * DH], w_in[:, :, bass.ds(i * DH + (COL_QB + g * 4 * DH), DH)]).then_inc(s_rawp[buf], 16)

        s_tick2, s_tick3, s_tick4 = sem("s_tick2"), sem("s_tick3"), sem("s_tick4")

        with nc.Block() as block:
            @block.sync
            def _(sp):
                with sp.Fori(1, 4) as it:
                    for j, col in enumerate((COL_QA, COL_KA, COL_VA, COL_GA, COL_GA + P)):
                        sp.wait_ge(s_split, it * 5 + j - 4)
                        sp.sem_inc(s_tick3, 1)
                        per_turn = 2 * P if j > 2 else P
                        sp.dma_start(raw_at[j], w_in[:, :, bass.ds(it * per_turn + col, P)]).then_inc(s_rawp[j], 16)
                for j, col in enumerate((COL_KS, COL_KW, COL_KCR, COL_VCR, COL_VS, COL_VW)):
                    load_piece(sp, KV_PIECE + j, w_in[:, :, col:col + P])
                for i, n in enumerate("kv"):
                    sp.dma_start(w1[i], a["cmp_w1_" + n][0].rearrange("(t p) n -> p t n", p=P)).then_inc(s_w1, 16)
                sp.wait_ge(s_split, before[B_PIECE(0, 0)])
                load_queries(sp, buf_of[B_PIECE(0, 0)], 0)
                for c in range(2):
                    load_piece(sp, B_PIECE(0, 1 + c), w_in[:, :, COL_GB + P * c:COL_GB + P * (c + 1)])

            @block.gpsimd
            def _(pool):
                for j in range(2, 5):
                    pool.wait_ge(s_w_hi, j + 1)
                    rest_of_piece(j, j)
                with pool.Fori(1, 4) as it:
                    for j in range(5):
                        pool.wait_ge(s_rawp[j], 16 * it + 16)
                        if j < 3:
                            pool.wait_ge(A["projected"], 3 * it + j - 2)
                        else:
                            pool.wait_ge(A["f_done"], 2 * it + j - 4)
                        pool.sem_inc(s_tick2, 1)
                        split_piece(pool, j, j)
                for j, slot in enumerate(SLOT_KV[:5]):
                    n = KV_PIECE + j
                    pool.wait_ge(s_rawp[buf_of[n]], landed[n])
                    if slot < 3:
                        pool.wait_ge(A["projected"], 12)
                    elif slot == 3:
                        pool.wait_ge(A["f_done"], 7)
                    split_piece(pool, buf_of[n], slot)

            @block.tensor
            def _(pe):
                pe.wait_ge(s_pos, 32)
                nc.tensor.transpose(bank[BT][:, 0:32], pos_rows, ident[0:32, 0:32]).then_inc(s_posT, 1)
                pe.wait_ge(s_posT, 2)
                with pe.Fori(0, 4) as it:
                    for i in range(2):
                        pe.wait_ge(s_split, it * 5 + i + 1)
                        pe.wait_ge(A["evicted"], 3 * it + 1)
                        wide_product(bank[BJ[i]][:, :], i).then_inc(A["projected"], 1)
                    pe.wait_ge(s_split, it * 5 + 3)
                    pe.wait_ge(A["evicted"], 3 * it + 2)
                    wide_product(bank[BJ[0]][:, :], 2).then_inc(A["projected"], 1)
                    pe.wait_ge(A["vT"], it + 1)
                    pe.wait_ge(A["evicted"], 3 * it + 3)
                    for t in range(NT):
                        last = nc.tensor.transpose(bank[BJ[1]][:, t * P:(t + 1) * P], pT[:, 0, t * P:(t + 1) * P], ident)
                    last.then_inc(A["v_rows"], 1)
                    pe.wait_ge(A["evicted"], 3 * it + 4)
                    attend_pe(pe, unitsA, fillA, it, A, lambda i, c: i * 5 + 3 + c)

            @block.vector
            def _(dve):
                dve.wait_ge(s_posT, 1)
                nc.vector.tensor_copy(pos2, bank[BT][:, 0:32])
                nc.vector.tensor_copy(pos2x[0:64], bank[BT][64:128, 0:32])
                nc.vector.tensor_copy(pos2x[64:128], bank[BT][0:64, 0:32]).then_inc(s_posT, 1)
                dve.wait_ge(s_cst, 16)
                dve.sem_inc(A["evicted"], 1)
                dve.sem_inc(A["f_evicted"], 1)
                dve.sem_inc(A["y_done"], 2)
                with dve.Fori(0, 4) as it:
                    nc.vector.tensor_copy(slope2[:, 0:2], C["slopes_a"][:, bass.ds(it * 2, 2)])
                    dve.drain()
                    for hh in range(2):
                        nc.vector.scalar_tensor_tensor(out=bias[:, hh, :], in0=C["dist"], scalar=slope2[:, hh:hh + 1],
                                                       in1=C["mdil"], op0=ALU.mult, op1=ALU.add)
                    dve.wait_ge(A["projected"], 3 * it + 1)
                    nc.vector.tensor_scalar(qT, bank[BJ[0]][:, :], -(DH ** -0.5), None, ALU.mult).then_inc(A["evicted"], 1)
                    dve.wait_ge(A["projected"], 3 * it + 2)
                    nc.vector.tensor_copy(kT[:, 0, :], bank[BJ[1]][:, :]).then_inc(A["evicted"], 1)
                    dve.wait_ge(A["v_rows"], it + 1)
                    nc.vector.tensor_copy(vvA, psv(BJ[1], NT, P)).then_inc(A["evicted"], 1)
                    dve.drain()

                    def put(dve, u, w):
                        dve.wait_ge(A["pv_done"], it * 8 + w + 1)
                        nc.vector.reciprocal(coef[:, w:w + 1], rowsum[:, w:w + 1])
                        dve.drain()
                        nc.vector.tensor_scalar(y[:, u["qt"], bass.ds(it * P + u["v"] * DH, DH)],
                                                bank[BV[u["group"] % 2]][:, 0:DH], coef[:, w:w + 1], None,
                                                ALU.mult).then_inc(A["y_done"], 1)

                    attend_dve(dve, unitsA, fillA, it, A, put, lambda c: gateT[:, it * 2 + c, :])

            @block.scalar
            def _(act):
                for j in range(2, 5):
                    round_first(act, j)
                with act.Fori(0, 4) as it:
                    act.wait_ge(A["projected"], 3 * it + 3)
                    act.sem_inc(s_tick4, 1)
                    nc.scalar.copy(pT[:, 0, :], bank[BJ[0]][:, :]).then_inc(A["vT"], 1)
                    attend_act(act, unitsA, it, A, lambda u, w: rowsum[:, w:w + 1])

        if "ya" in dbg:
            dump(nc, sem("d2"), dbg["ya"], y[:, :, 0:512])

        def blocks_of(i, half):
            return y[:, 2 * i + half, 512:512 + 16 * NC].rearrange("p (t g n) -> p t g n", t=8, g=2)

        def load_merge_piece(sp, m):
            n = WM_PIECE + m
            sp.wait_ge(s_split, before[n])
            for i, name in enumerate("ab"):
                sp.dma_start(raw_at[buf_of[n]][:, 4 * i:4 * i + 4, :],
                             a["w_branch_" + name][0].rearrange("(k p) n -> p k n", p=P)[:, :, m * P:(m + 1) * P]).then_inc(s_rawp[buf_of[n]], 16)

        def load_out_piece(sp, j):
            c = WO[j][0]
            load_piece(sp, WO_PIECE + j, chunks(a["w_out"][0])[:, :, c * P:(c + 1) * P])

        with nc.Block() as block:
            @block.sync
            def _(sp):
                sp.wait_ge(s_hid, 1)
                sp.dma_start(h[:, :, :], a["x"][0].rearrange("(t p) n -> p t n", p=P)).then_inc(s_xagain, 16)
                with sp.Fori(1, 4) as it:
                    sp.wait_ge(s_split, it * 3 + 24)
                    sp.sem_inc(s_tick3, 1)
                    load_queries(sp, 4, it)
                    for c in range(2):
                        sp.wait_ge(s_split, it * 3 + 25 + c)
                        sp.sem_inc(s_tick3, 1)
                        sp.dma_start(raw_at[c], w_in[:, :, bass.ds(it * 256 + (COL_GB + P * c), P)]).then_inc(s_rawp[c], 16)
                for m in range(KD):
                    load_merge_piece(sp, m)
                for j in range(2):
                    load_out_piece(sp, j)

            @block.gpsimd
            def _(pool):
                n = KV_PIECE + 5
                pool.wait_ge(s_rawp[buf_of[n]], landed[n])
                split_piece(pool, buf_of[n], SLOT_KV[5])
                pool.wait_ge(B["projected"], 1)
                n = B_PIECE(0, 0)
                pool.wait_ge(s_rawp[buf_of[n]], landed[n])
                split_piece(pool, buf_of[n], SLOT_KV[0])
                for c in range(2):
                    n = B_PIECE(0, 1 + c)
                    pool.wait_ge(s_rawp[buf_of[n]], landed[n])
                    pool.wait_ge(B["projected"], 5)
                    split_piece(pool, buf_of[n], SLOT_GATE + c)
                with pool.Fori(1, 4) as it:
                    pool.wait_ge(s_rawp[4], it * 32 + landed[B_PIECE(1, 0)] - 32)
                    pool.wait_ge(B["projected"], it + 7)
                    pool.sem_inc(s_tick2, 1)
                    split_piece(pool, 4, SLOT_KV[0])
                    for c in range(2):
                        pool.wait_ge(s_rawp[c], it * 16 + landed[B_PIECE(1, 1 + c)] - 16)
                        pool.wait_ge(B["f_done"], it * 2 + c - 1)
                        pool.sem_inc(s_tick2, 1)
                        split_piece(pool, c, SLOT_GATE + c)
                for m in range(5):
                    n = WM_PIECE + m
                    pool.wait_ge(s_rawp[buf_of[n]], landed[n])
                    if SLOT_WM[m] == SLOT_KV[0]:
                        pool.wait_ge(B["projected"], 11)
                    elif SLOT_WM[m] == SLOT_GATE:
                        pool.wait_ge(B["f_done"], 7)
                    split_piece(pool, buf_of[n], SLOT_WM[m])

            @block.tensor
            def _(pe):
                pe.wait_ge(s_hg, 2)
                n = 0
                for k in range(KD):
                    for zx, zw in PASSES:
                        last = nc.tensor.matmul(bank[BS[0]][0:24, :], gn_hl[:, zw, k, :], x_hl[:, zx, k, :], start=n == 0, stop=n == 3 * KD - 1)
                        n += 1
                last.then_inc(s_hg, 1)
                for i in range(4):
                    pe.wait_ge(s_split, KV_PIECE + i + 1)
                    if i >= 2:
                        pe.wait_ge(B["evicted"], i - 1)
                    wide_product(bank[BJ[i % 2]][:, :], SLOT_KV[i]).then_inc(B["projected"], 1)
                pe.wait_ge(s_split, KV_PIECE + 6)
                for t in range(NT):
                    out = bank[BV[t // 2]][:, (t % 2) * 256:(t % 2 + 1) * 256]
                    n = 0
                    for k in range(KD):
                        for zx, zw in PASSES:
                            last = nc.tensor.matmul(out, x_hl[:, zx, k, t * P:(t + 1) * P], w_hl[:, 3:5, zw, k, :],
                                                    start=n == 0, stop=n == 3 * KD - 1)
                            n += 1
                last.then_inc(B["projected"], 1)
                pe.wait_ge(s_hg, 4)
                for t in range(NT):
                    last = nc.tensor.transpose(bank[BT][:, t * 24:(t + 1) * 24], gnT[:, t * P:(t + 1) * P], ident[0:24, 0:24])
                last.then_inc(s_hg, 1)
                pe.wait_ge(s_w1, 32)
                pe.wait_ge(s_w2, 80)
                for i in range(2):
                    pe.wait_ge(B["evicted"], 3 + i)
                    for c in range(2):
                        for t in range(16):
                            last = nc.tensor.matmul(bank[BJ[i]][:, c * 64:c * 64 + 2 * NC], w1[i][:, t, c * P:(c + 1) * P],
                                                    blocks_of(i, t // 8)[:, t % 8].rearrange("p g n -> p (g n)"), start=t == 0, stop=t == 15)
                    last.then_inc(s_hid, 1)
                pe.wait_ge(s_gelu, 2)
                for c in range(2):
                    last = nc.tensor.matmul(bank[BS[1]][:, 0:2 * NC], w2[:, c, 0:P], hTc[:, 0, c, :], start=c == 0, stop=c == 1)
                last.then_inc(B["projected"], 1)
                pe.wait_ge(s_gelu, 4)
                for g in range(2):
                    for c in range(2):
                        last = nc.tensor.matmul(bank[BF][0:NC, P + g * DH:P + (g + 1) * DH], hTc[:, 1, c, g * NC:(g + 1) * NC],
                                                w2[:, c, P:P + DH], start=c == 0, stop=c == 1)
                last.then_inc(B["projected"], 1)
                with pe.Fori(0, 4) as it:
                    pe.wait_ge(s_split, it * 3 + 27)
                    pe.wait_ge(B["evicted"], it + 7)
                    wide_product(bank[BJ[0]][:, :], SLOT_KV[0]).then_inc(B["projected"], 1)
                    pe.wait_ge(B["evicted"], it + 8)
                    attend_pe(pe, unitsB, fillB, it, B, lambda i, c: i * 3 + 27 + c)

            @block.vector
            def _(dve):
                dve.wait_ge(s_hg, 1)
                nc.vector.tensor_tensor(gn_hl[:, 1], gn_w, gn_hl[:, 0].bitcast(F32), ALU.subtract).then_inc(s_hg, 1)
                dve.sem_inc(B["f_evicted"], 1)
                dve.sem_inc(B["y_done"], 2)
                for i in range(2):
                    dve.wait_ge(B["projected"], i + 1)
                    nc.vector.tensor_copy(kT[:, i, :], bank[BJ[i]][:, :]).then_inc(B["evicted"], 1)
                for i in range(2):
                    dve.wait_ge(B["projected"], 3 + i)
                    raw_kv = bank[BJ[i]][:, :].rearrange("p (n t two) -> p two t n", t=8, two=2)
                    for half in range(2):
                        for par in range(2):
                            for g in range(2):
                                src = slice(64 * g, 64 * g + 64)
                                pos = (pos2 if g == par else pos2x)[src, 16 * i + 8 * half:16 * i + 8 * half + 8]
                                last = nc.vector.tensor_tensor(blocks_of(i, half)[64 * par:64 * par + 64, :, g], raw_kv[src, par, :, half:half + NC],
                                                               pos.unsqueeze(2).to_broadcast([64, 8, NC]), ALU.add)
                    last.then_inc(B["evicted"], 1)
                dve.wait_ge(B["projected"], 5)
                for j in range(2):
                    last = nc.vector.tensor_copy(vvB[:, 2 * j:2 * j + 2, :], psv(BV[j], 2, 256))
                last.then_inc(B["evicted"], 1)
                dve.wait_ge(B["projected"], 6)
                for g in range(2):
                    last = nc.vector.tensor_copy(kcT[64 * g:64 * g + 64, 0:NC], bank[BS[1]][64 * g:64 * g + 64, g * NC:(g + 1) * NC])
                last.then_inc(B["evicted"], 1)
                dve.wait_ge(B["projected"], 7)
                nc.vector.tensor_copy(vc_sb[0:NC, :], bank[BF][0:NC, P:2 * P]).then_inc(B["evicted"], 1)
                dve.wait_ge(s_hg, 6)
                with dve.Fori(0, 4) as it:
                    nc.vector.tensor_copy(slope2[:, 0:2], C["slopes_b"].rearrange("p (g i) -> p g i", g=2)[:, :, bass.ds(it, 1)].rearrange("p g i -> p (g i)"))
                    nc.vector.tensor_copy(gts.rearrange("p t b n -> p (t b n)"), gates.rearrange("p t (b i) -> p (t b) i", i=4)[:, :, bass.ds(it, 1)].rearrange("p a i -> p (a i)"))
                    dve.drain()
                    for i in range(2):
                        nc.vector.scalar_tensor_tensor(out=bias[:, i, :], in0=C["dist"], scalar=slope2[:, i:i + 1],
                                                       in1=C["mfull"], op0=ALU.mult, op1=ALU.add)
                        nc.vector.scalar_tensor_tensor(out=bias_c[:, i].rearrange("p t n -> p (t n)"), in0=C["dcmp"],
                                                       scalar=slope2[:, i:i + 1], in1=C["mcmp"], op0=ALU.mult, op1=ALU.add)
                    dve.wait_ge(B["projected"], it + 8)
                    nc.vector.tensor_scalar(qT, bank[BJ[0]][:, :], -(DH ** -0.5), None, ALU.mult).then_inc(B["evicted"], 1)
                    dve.drain()

                    def put(dve, u, w):
                        g, b = u["group"] // NT, u["group"] % 2
                        c = coef[:, 4 * b:4 * b + 3]
                        bk = bank[BV[b]]
                        dve.wait_ge(B["pv_done"], it * 24 + w + 1)
                        nc.vector.tensor_scalar(c, rsum3[:, b, :], 0.5, None, ALU.max)
                        dve.drain()
                        nc.vector.reciprocal(c, c)
                        dve.drain()
                        nc.vector.tensor_tensor(c, c, gts[:, u["qt"], :, g], ALU.mult)
                        dve.drain()
                        dst = y[:, u["qt"], bass.ds(it * DH + (WIDTH_A + g * 4 * DH), DH)]
                        nc.vector.tensor_scalar(ysum[:, b, 0, :], bk[:, 0:DH], c[:, 0:1], None, ALU.mult)
                        dve.drain()
                        nc.vector.scalar_tensor_tensor(out=ysum[:, b, 1, :], in0=bk[:, DH:2 * DH], scalar=c[:, 1:2],
                                                       in1=ysum[:, b, 0, :], op0=ALU.mult, op1=ALU.add)
                        dve.drain()
                        nc.vector.scalar_tensor_tensor(out=dst, in0=bk[:, 2 * DH:3 * DH], scalar=c[:, 2:3],
                                                       in1=ysum[:, b, 1, :], op0=ALU.mult, op1=ALU.add).then_inc(B["y_done"], 1)

                    attend_dve(dve, unitsB, fillB, it, B, put, lambda c: gateT[:, it * 2 + KD + c, :])

            @block.scalar
            def _(act):
                act.wait_ge(s_gn, 16)
                nc.scalar.copy(gn_hl[:, 0], gn_w).then_inc(s_hg, 1)
                act.wait_ge(s_hg, 3)
                nc.scalar.copy(gnT, bank[BS[0]][0:24, :]).then_inc(s_hg, 1)
                act.wait_ge(s_hg, 5)
                nc.scalar.activation(gates, psv(BT, NT, 24), ACT.Sigmoid).then_inc(s_hg, 1)
                for i in range(2):
                    act.wait_ge(s_hid, i + 1)
                    for c in range(2):
                        nc.scalar.activation(hTc[:, i, c, :], bank[BJ[i]][:, c * 64:c * 64 + 2 * NC], ACT.Gelu_apprx_tanh,
                                             bias=b1c[:, 2 * i + c:2 * i + c + 1]).then_inc(s_gelu, 1)
                with act.Fori(0, 4) as it:
                    attend_act(act, unitsB, it, B, lambda u, w: rsum3[:, u["group"] % 2, u["br"]:u["br"] + 1])

        if "yb" in dbg:
            dump(nc, sem("d3"), dbg["yb"], y[:, :, 512:1024])

        mT = gateT[:, 0:KD]
        wsg = r1[:, 0:4096].rearrange("p (i k n) -> p i k n", i=2, k=KD)
        xn2T = gateT[:, 0:KD, :]
        wr = gateT[:, KD, 0:512].rearrange("p (k n) -> p k n", k=KD)
        rb = gateT[:, KD + 1, 0:NE]
        gbc2 = gateT[:, KD + 2:KD + 4, :].rearrange("p a b -> p (a b)")
        wsd = [gateT[:, KD + 2:KD + 4, :].rearrange("p a b -> p (a b)"), work[:, WORK - D:WORK]]
        xpart = small[:, 96:104]
        NEP = NE + NPAD
        at = [0]

        def wk(n, *dims):
            v = work[:, at[0]:at[0] + n]
            at[0] += n
            if len(dims) == 2:
                return v.rearrange("p (a b) -> p a b", a=dims[0])
            if len(dims) == 3:
                return v.rearrange("p (a b c) -> p a b c", a=dims[0], b=dims[1])
            return v

        posm = wk(NEP * NT, NEP, NT)
        LIST = 6
        tokw = wk(NEP * NT * LIST // 2).bitcast(BF16).rearrange("p (a b c) -> p a b c", a=NEP, b=NT)
        wts = wk(NEP)
        dstf = wk(NEP)
        didx = wk(2).bitcast(I32)
        etab = wk(NOV).bitcast(I32)
        ntot = wk(1).bitcast(I32)
        many = small[:, 188:188 + NEP].bitcast(I32)
        q128 = wk(NOV)
        idx = wk(2).bitcast(I32)
        onehot = wk(NT * CAP // 2).bitcast(BF16).rearrange("p (a b) -> p a b", a=NT)
        listed, place2 = wk(LIST), wk(2)
        sg, hid = wk(EH), wk(EH)
        hT = wk(2 * CAP, 2, CAP)
        at_moe = at[0]
        sco, sel, selm, rep, mask, wn, pos1 = (wk(NT * NE, NT, NE) for _ in range(7))
        g8 = wk(NT * NG * 8, NT * NG, 8)
        gs, gm, gneg, rank = (wk(NT * NG, NT, NG) for _ in range(4))
        m8 = wk(NT * 8, NT, 8)
        wsum = wk(NT)
        novT = wk(P)
        ovs, nov, oven = (wk(NE) for _ in range(3))
        rank2 = wk(NOV)
        assert at[0] <= WORK - D, at[0]
        big = gateT[:, KD + 4:KD + 8, :].rearrange("p a b -> p (a b)")
        pair = big[:, 0:NT * NG * NG].rearrange("p (t a b) -> p t a b", t=NT, a=NG)
        pair2 = big[:, 256:256 + NT * NG * NG].rearrange("p (t a b) -> p t a b", t=NT, a=NG)
        jcmp = big[:, 0:NOV * NE].rearrange("p (j e) -> p j e", j=NOV)
        shid = y

        cn = "yt_done yt_hi yt_lo sig merged_pe merged mt_hi mt_lo wo_done h_done ms rr xn stored xt_done xt_dve xt_act r_done sco mask lists gu_done silu hid hT_pe hT dn_done dn_out".split()
        M = {n: sem("m_" + n) for n in cn}
        s_ws, s_wr, s_g2 = sem("s_ws"), sem("s_wr"), sem("s_g2")
        s_raw = [[sem(f"s_raw{b}_{n}") for n in ("gate", "up")] for b in range(2)]
        s_wd = [sem("s_wd0"), sem("s_wd1")]
        assert at_moe <= WORK - 4096, at_moe
        raw = [v.rearrange("p (i n) -> p i n", i=2) for v in (r1[:, 0:4096], work[:, WORK - 4096:WORK])]
        xg = [r1[:, 4096 + b * D:4096 + (b + 1) * D] for b in range(2)]
        Wd = [y[:, 2 * b:2 * b + 2, :] for b in range(2)]

        xg_f = [sem(f"s_xg{b}") for b in range(2)]
        stored = [sem(f"s_stored{b}") for b in range(2)]
        row_free = sem("s_row_free")
        dn = "oh list idx xt_pe xt_hi xt_lo hi lo gu silu hid hT_pe hT dn o_dve o_act".split()
        E = {n: sem("e_" + n) for n in dn}
        s_xz, s_tick5 = sem("s_xz"), sem("s_tick5")
        BL, BX, BH, BT2, BO = 0, (1, 2), 3, 4, (5, 6)

        def list_products(pe, e, s, out=bank[0]):
            for t in range(NT):
                last = nc.tensor.matmul(out[:, 0:LIST], onehot[:, t, :], tokw[:, e, t, :], start=t == 0, stop=t == NT - 1)
            last.then_inc(s["list"], 1)

        def one_hot(e):
            nc.vector.tensor_tensor(onehot, C["slot"].unsqueeze(1).to_broadcast([P, NT, CAP]),
                                    posm[:, e, :].unsqueeze(2).to_broadcast([P, NT, CAP]), ALU.is_equal).then_inc(E["oh"], 1)

        def take_numbers(dve, src, to_idx, to_dst, to_wts, taken):
            nc.vector.tensor_copy(listed, src[:, 0:LIST])
            dve.drain()
            nc.vector.scalar_tensor_tensor(out=place2[:, 0:1], in0=listed[:, 0:1], scalar=float(S), in1=listed[:, 1:2], op0=ALU.add, op1=ALU.add)
            nc.vector.tensor_tensor(place2[:, 1:2], listed[:, 3:4], listed[:, 4:5], ALU.add)
            dve.drain()
            nc.vector.tensor_copy(to_idx, place2[:, 0:1]).then_inc(taken, 1)
            nc.vector.scalar_tensor_tensor(out=to_dst, in0=place2[:, 0:1], scalar=8.0, in1=listed[:, 2:3], op0=ALU.mult, op1=ALU.add)
            nc.vector.tensor_tensor(to_wts, place2[:, 1:2], listed[:, 5:6], ALU.add)

        def take_list(dve, e, b, src=bank[0]):
            dve.wait_ge(E["list"], e + 1)
            dve.sem_inc(s_tick5, 1)
            take_numbers(dve, src, idx[:, b:b + 1], dstf[:, bass.ds(e, 1)], wts[:, bass.ds(e, 1)], E["idx"])

        def by_length(pool, e, move):
            length = pool.value_load(many[0:1, bass.ds(e, 1)], min_val=0, max_val=S)
            for lo, n in zip((-1,) + MOVES, MOVES):
                with pool.If(length > lo):
                    with pool.If(length < (n if n < CAP else S) + 1):
                        move(n)

        def gather(pool, e, b):
            by_length(pool, e, lambda n: pool.indirect_dma_start(
                out=xg[b][0:n, :], out_offset=None, in_=xn2_d, in_offset=bass.IndirectOffsetOnAxis(ap=idx[0:n, b:b + 1], axis=0),
                bounds_check=S - 1, oob_is_err=False).then_inc(xg_f[b], 16))

        def load_gu(sp, e, b, i):
            w = a[("w_gate", "w_up")[i]][0].rearrange("e (p k) n -> e p (k n)", k=KD)
            sp.dma_start(raw[b][:, i, :], w[e]).then_inc(s_raw[b][i], 16)

        with nc.Block() as block:
            @block.sync
            def _(sp):
                for j in range(2, KD):
                    load_out_piece(sp, j)
                sp.wait_ge(M["merged"], KD)
                sp.dma_start(wr, chunks(a["w_router"][0])).then_inc(s_wr, 16)
                sp.dma_start(rb, a["router_bias"][0].partition_broadcast(P)).then_inc(s_wr, 16)
                sp.dma_start(gbc2, a["g_ffn"][0].partition_broadcast(P)).then_inc(s_g2, 16)
                sp.wait_ge(s_split, WO_PIECE + KD)
                for i, n in enumerate(("ws_gate", "ws_up")):
                    sp.dma_start(wsg[:, i], chunks(a[n][0])).then_inc(s_ws, 16)
                for t in range(NT):
                    sp.wait_ge(M["xn"], t + 1)
                    sp.dma_start(xn2_d[t * P:(t + 1) * P, :], y[:, t, :]).then_inc(M["stored"], 16)
                for c in range(2):
                    sp.dma_start(wsd[c], a["ws_down"][0].rearrange("(c p) n -> p c n", p=P)[:, c]).then_inc(s_g2, 16)
                sp.wait_ge(M["gu_done"], NT)
                for i in range(2):
                    load_gu(sp, 0, 0, i)

            @block.gpsimd
            def _(pool):
                for n in range(WM_PIECE + 5, WO_PIECE + KD):
                    pool.wait_ge(s_w_hi, n - WM_PIECE + 1)
                    rest_of_piece(buf_of[n], SLOT_OF[n - WM_PIECE])
                for t in range(NT):
                    pool.wait_ge(M["ms"], t + 1)
                    nc.gpsimd.tensor_tensor(xpart[:, 4 + t:5 + t], xpart[:, t:t + 1], C["nhalf"][:, 0:1], ALU.pow).then_inc(M["rr"], 1)
                for b in range(2):
                    nc.gpsimd.memset(xg[b], 0.0).then_inc(s_xz, 1)
                pool.wait_ge(s_xz, 2)
                pool.wait_ge(M["stored"], 16 * NT)
                for b in range(2):
                    pool.wait_ge(E["idx"], b + 1)
                    gather(pool, b, b)

            @block.tensor
            def _(pe):
                for k in range(KD):
                    for t in range(NT):
                        last = nc.tensor.transpose(bank[k][:, t * P:(t + 1) * P], y[:, t, k * P:(k + 1) * P], ident)
                    last.then_inc(M["yt_done"], 1)
                pe.wait_ge(M["yt_lo"], KD)
                for m in range(KD):
                    pe.wait_ge(s_split, WM_PIECE + m + 1)
                    if m >= 4:
                        pe.wait_ge(M["merged"], m - 3)
                    for i in range(2):
                        for k in range(4 * i, 4 * i + 4):
                            for j, (zx, zw) in enumerate(PASSES):
                                last = nc.tensor.matmul(bank[2 * (m % 4) + i][:, :], w_hl[:, SLOT_OF[m], zw, k, :], x_hl[:, zx, k, :],
                                                        start=k % 4 + j == 0, stop=k % 4 == 3 and j == 2)
                    last.then_inc(M["merged_pe"], 1)

                def out_proj(t, q):
                    lo = (2, 4, 0, 2)[q]
                    n = 0
                    for k in range(KD):
                        if t == q == 0:
                            pe.wait_ge(M["mt_lo"], k + 1)
                        for zx, zw in PASSES:
                            last = nc.tensor.matmul(bank[t][:, (q % 2) * 256:(q % 2 + 1) * 256], x_hl[:, zx, k, t * P:(t + 1) * P],
                                                    w_hl[:, lo:lo + 2, zw, k, :], start=n == 0, stop=n == 3 * KD - 1)
                            n += 1
                    last.then_inc(M["wo_done"], 1)

                def transpose_xn(t):
                    pe.wait_ge(M["xn"], t + 1)
                    if t:
                        pe.wait_ge(M["xt_dve"], t)
                        pe.wait_ge(M["xt_act"], t)
                    for k in range(KD):
                        last = nc.tensor.transpose(bank[4 + k // 4][:, (k % 4) * P:(k % 4 + 1) * P],
                                                   y[:, t, k * P:(k + 1) * P], ident)
                    last.then_inc(M["xt_done"], 1)

                def router(t):
                    pe.wait_ge(M["xt_dve"], t + 1)
                    pe.wait_ge(M["xt_act"], t + 1)
                    for k in range(KD):
                        last = nc.tensor.matmul(bank[6][:, t * NE:(t + 1) * NE], xn2T[:, k, t * P:(t + 1) * P], wr[:, k, :],
                                                start=k == 0, stop=k == KD - 1)
                    last.then_inc(M["r_done"], 1)

                def shared_up(t):
                    for k in range(KD):
                        last = nc.tensor.matmul(bank[t][:, :], xn2T[:, k, t * P:(t + 1) * P], wsg[:, :, k, :],
                                                start=k == 0, stop=k == KD - 1)
                    last.then_inc(M["gu_done"], 1)

                pe.wait_ge(s_split, WO_PIECE + 4)
                pe.wait_ge(M["merged"], KD)
                for q in range(2):
                    for t in range(NT):
                        out_proj(t, q)
                pe.wait_ge(s_split, WO_PIECE + KD)
                for t in range(NT):
                    pe.wait_ge(M["h_done"], t + 1)
                    for q in (2, 3):
                        out_proj(t, q)
                    if t:
                        transpose_xn(t - 1)
                        if t == 1:
                            pe.wait_ge(s_wr, 32)
                        router(t - 1)
                pe.wait_ge(M["h_done"], NT + 1)
                pe.wait_ge(s_ws, 32)
                shared_up(0)
                transpose_xn(3)
                router(3)
                pe.wait_ge(M["h_done"], 2 * NT)
                shared_up(1)
                shared_up(2)
                pe.wait_ge(M["mask"], 1)
                for t in range(NT):
                    for u in range(t + 1):
                        last = nc.tensor.matmul(bank[7][:, t * NE:(t + 1) * NE], C["tri"] if u == t else C["ones"],
                                                mask[:, u, :], start=u == 0, stop=u == t)
                last.then_inc(M["lists"], 1)
                pe.wait_ge(M["lists"], 2)
                for t in range(NT):
                    last = nc.tensor.matmul(bank[7][0:NE, 0:P], mask[:, t, :], C["ones"], start=t == 0, stop=t == NT - 1)
                for t in range(NT):
                    last = nc.tensor.matmul(bank[7][:, 384:384 + NE], C["ones"], mask[:, t, :], start=t == 0, stop=t == NT - 1)
                last.then_inc(M["lists"], 1)
                pe.wait_ge(E["oh"], 1)
                list_products(pe, 0, E, bank[4])
                shared_up(3)
                pe.wait_ge(E["oh"], 2)
                list_products(pe, 1, E, bank[4])
                pe.wait_ge(M["lists"], 4)
                nc.tensor.matmul(bank[7][:, 128:128 + NE], novT[0:NE, :], C["tri64"][0:NE, :], start=True, stop=True)
                nc.tensor.matmul(bank[7][:, 256:256 + NE], novT[0:NE, :], ident[0:NE, 0:NE], start=True, stop=True).then_inc(M["lists"], 1)
                for t in range(NT):
                    pe.wait_ge(M["hid"], t + 1)
                    if t == 0:
                        pe.wait_ge(E["idx"], 2)
                        pe.wait_ge(s_g2, 48)
                    for c in range(2):
                        last = nc.tensor.transpose(bank[4][:, c * P:(c + 1) * P], shid[:, t, c * P:(c + 1) * P], ident)
                    last.then_inc(M["hT_pe"], 1)
                    pe.wait_ge(M["hT"], t + 1)
                    if t >= 2:
                        pe.wait_ge(M["dn_out"], 2 * (t - 1))
                    for i in range(2):
                        for c in range(2):
                            last = nc.tensor.matmul(bank[5 + i if t % 2 == 0 else i][:, :], shid[:, t, 512 + c * P:512 + (c + 1) * P],
                                                    wsd[c][:, i * 512:(i + 1) * 512], start=c == 0, stop=c == 1)
                    last.then_inc(M["dn_done"], 1)

            @block.scalar
            def _(act):
                for k in range(KD):
                    act.wait_ge(M["yt_done"], k + 1)
                    nc.scalar.copy(x_hl[:, 0, k, :], bank[k][:, :]).then_inc(M["yt_hi"], 1)

                def round_piece(n):
                    act.wait_ge(s_rawp[buf_of[n]], landed[n])
                    nc.scalar.copy(w_hl[:, SLOT_OF[n - WM_PIECE], 0], raw_at[buf_of[n]]).then_inc(s_w_hi, 1)

                def gate(m):
                    nc.scalar.activation(gateT[:, m, :], gateT[:, m, :], ACT.Sigmoid)
                    nc.scalar.activation(gateT[:, KD + m, :], gateT[:, KD + m, :], ACT.Sigmoid).then_inc(M["sig"], 1)

                round_piece(WM_PIECE + 5)
                for m in range(4):
                    gate(m)
                for m in range(KD):
                    act.wait_ge(M["merged_pe"], m + 1)
                    round_piece(WM_PIECE + 6 + m)
                    if m < 4:
                        gate(m + 4)
                act.wait_ge(M["merged"], KD)
                for k in range(KD):
                    nc.scalar.copy(x_hl[:, 0, k, :], mT[:, k, :]).then_inc(M["mt_hi"], 1)
                act.wait_ge(M["wo_done"], NT)
                round_piece(WO_PIECE + 6)
                round_piece(WO_PIECE + 7)
                for t in range(NT):
                    act.wait_ge(M["xt_done"], t + 1)
                    nc.scalar.copy(xn2T[:, 4:8, t * P:(t + 1) * P], psv(5, 4, P)).then_inc(M["xt_act"], 1)
                act.wait_ge(M["r_done"], NT)
                nc.scalar.activation(sco, psv(6, NT, NE), ACT.Sigmoid).then_inc(M["sco"], 1)
                act.wait_ge(M["stored"], 16 * NT)
                for t in range(NT):
                    act.wait_ge(M["gu_done"], t + 1)
                    nc.scalar.activation(shid[:, t, 256:512], bank[t][:, 0:EH], ACT.Silu).then_inc(M["silu"], 1)
                for t in range(NT):
                    act.wait_ge(M["hT_pe"], t + 1)
                    nc.scalar.copy(shid[:, t, 512:768], bank[4][:, 0:256]).then_inc(M["hT"], 1)

            @block.vector
            def _(dve):
                for k in range(KD):
                    dve.wait_ge(M["yt_hi"], k + 1)
                    nc.vector.tensor_tensor(x_hl[:, 1, k, :], bank[k][:, :], x_hl[:, 0, k, :].bitcast(F32), ALU.subtract).then_inc(M["yt_lo"], 1)
                for m in range(KD):
                    dve.wait_ge(M["sig"], m + 1)
                    dve.wait_ge(M["merged_pe"], m + 1)
                    nc.vector.tensor_tensor(gateT[:, m, :], gateT[:, m, :], bank[2 * (m % 4)][:, :], ALU.mult)
                    nc.vector.tensor_tensor(gateT[:, KD + m, :], gateT[:, KD + m, :], bank[2 * (m % 4) + 1][:, :], ALU.mult)
                    dve.drain()
                    nc.vector.tensor_tensor(mT[:, m, :], gateT[:, m, :], gateT[:, KD + m, :], ALU.add).then_inc(M["merged"], 1)
                for k in range(KD):
                    dve.wait_ge(M["mt_hi"], k + 1)
                    nc.vector.tensor_tensor(x_hl[:, 1, k, :], mT[:, k, :], x_hl[:, 0, k, :].bitcast(F32), ALU.subtract).then_inc(M["mt_lo"], 1)
                dve.wait_ge(s_xagain, 16)
                dve.wait_ge(s_g2, 16)
                for t in range(NT):
                    dve.wait_ge(M["wo_done"], NT + t + 1)
                    nc.vector.tensor_tensor(h[:, t, 0:512], h[:, t, 0:512], bank[t][:, :], ALU.add).then_inc(M["h_done"], 1)
                for t in range(NT):
                    dve.wait_ge(M["wo_done"], 2 * NT + 2 * t + 2)
                    nc.vector.tensor_tensor(h[:, t, 512:1024], h[:, t, 512:1024], bank[t][:, :], ALU.add).then_inc(M["h_done"], 1)
                    dve.drain()
                    norm_sums(dve, t, h[:, t, :], y[:, t, :], xpart).then_inc(M["ms"], 1)
                    dve.wait_ge(M["rr"], t + 1)
                    nc.vector.scalar_tensor_tensor(out=y[:, t, :], in0=h[:, t, :], scalar=xpart[:, 4 + t:5 + t], in1=gbc2,
                                                   op0=ALU.mult, op1=ALU.mult).then_inc(M["xn"], 1)
                    dve.wait_ge(M["xt_done"], t + 1)
                    nc.vector.tensor_copy(xn2T[:, 0:4, t * P:(t + 1) * P], psv(4, 4, P)).then_inc(M["xt_dve"], 1)
                nc.vector.memset(posm[:, NE:NEP, :], -1.0)
                nc.vector.memset(tokw[:, NE:NEP], 0.0)
                nc.vector.tensor_copy(tokw[:, 0:NE, :, 0], C["tok_a"].unsqueeze(1).to_broadcast([P, NE, NT]))
                nc.vector.tensor_copy(tokw[:, 0:NE, :, 1], C["tok_b"].unsqueeze(1).to_broadcast([P, NE, NT]))
                dve.wait_ge(M["sco"], 1)
                dve.wait_ge(s_wr, 32)
                nc.vector.tensor_tensor(sel, sco, rb.unsqueeze(1).to_broadcast([P, NT, NE]), ALU.add)
                dve.drain()
                for j in range(NT * NG):
                    nc.vector.max(g8[:, j, :], sel[:, j // NG, (j % NG) * 8:(j % NG + 1) * 8])
                dve.drain()
                gs_ = gs.rearrange("p t g -> p (t g)")
                nc.vector.tensor_tensor(gs_, g8[:, :, 0], g8[:, :, 1], ALU.add)
                dve.drain()
                mine = gs.unsqueeze(3).to_broadcast([P, NT, NG, NG])
                other = gs.unsqueeze(2).to_broadcast([P, NT, NG, NG])
                before = C["before8"].rearrange("p (a b) -> p a b", a=NG).unsqueeze(1).to_broadcast([P, NT, NG, NG])
                nc.vector.tensor_tensor(pair, other, mine, ALU.is_gt)
                nc.vector.tensor_tensor(pair2, other, mine, ALU.is_equal)
                dve.drain()
                nc.vector.tensor_tensor(pair2, pair2, before, ALU.mult)
                dve.drain()
                nc.vector.tensor_tensor(pair, pair, pair2, ALU.add)
                dve.drain()
                nc.vector.tensor_reduce(rank, pair, axis=AX_X, op=ALU.add)
                dve.drain()
                nc.vector.tensor_scalar(gm, rank, 4.0, None, ALU.is_lt)
                dve.drain()
                nc.vector.tensor_scalar(gneg, gm, 1.0, BIG, ALU.subtract, ALU.mult)
                each = lambda v: v.rearrange("p t g -> p (t g)").unsqueeze(2).to_broadcast([P, NT * NG, 8])
                flat8 = lambda v: v.rearrange("p t (g e) -> p (t g) e", g=NG)
                nc.vector.tensor_tensor(flat8(selm), flat8(sel), each(gm), ALU.mult)
                dve.drain()
                nc.vector.tensor_tensor(flat8(selm), flat8(selm), each(gneg), ALU.add)
                dve.drain()
                for t in range(NT):
                    nc.vector.max(m8[:, t, :], selm[:, t, :])
                dve.drain()
                for t in range(NT):
                    nc.vector.match_replace(out=rep[:, t, :], in_to_replace=m8[:, t, :], in_values=selm[:, t, :], imm_value=-2.0 * BIG)
                dve.drain()
                nc.vector.tensor_tensor(mask, rep, selm, ALU.not_equal).then_inc(M["mask"], 1)
                dve.drain()
                nc.vector.tensor_tensor(wn, sco, mask, ALU.mult)
                dve.drain()
                nc.vector.tensor_reduce(wsum, wn, axis=AX_X, op=ALU.add)
                dve.drain()
                nc.vector.reciprocal(wsum, wsum)
                dve.drain()
                nc.vector.tensor_scalar(wsum, wsum, ROUTED_SCALE, None, ALU.mult)
                dve.drain()
                nc.vector.tensor_tensor(wn, wn, wsum.unsqueeze(2).to_broadcast([P, NT, NE]), ALU.mult)
                for c in range(3):
                    part_c = tokw[:, 0:NE, :, 3 + c].rearrange("p e t -> p t e")
                    dve.drain()
                    nc.vector.tensor_copy(part_c, wn)
                    if c < 2:
                        dve.drain()
                        nc.vector.tensor_tensor(wn, wn, part_c, ALU.subtract)
                src, dst = mask, sel
                for n in (1, 2, 4, 8, 16, 32):
                    nc.vector.tensor_tensor(dst[:, :, n:NE], src[:, :, n:NE], src[:, :, 0:NE - n], ALU.add)
                    nc.vector.tensor_copy(dst[:, :, 0:n], src[:, :, 0:n])
                    dve.drain()
                    src, dst = dst, (selm if dst is sel else sel)
                nc.vector.tensor_scalar(tokw[:, 0:NE, :, 2].rearrange("p e t -> p t e"), src, 1.0, None, ALU.subtract)
                dve.wait_ge(M["lists"], 1)
                nc.vector.tensor_scalar(pos1, psv(7, NT, NE), 1.0, None, ALU.add).then_inc(M["lists"], 1)
                dve.drain()
                nc.vector.tensor_tensor(rep, pos1, mask, ALU.mult)
                dve.drain()
                nc.vector.tensor_scalar(posm[:, 0:NE, :].rearrange("p e t -> p t e"), rep, 1.0, None, ALU.subtract)
                dve.drain()
                one_hot(0)
                dve.wait_ge(M["lists"], 3)
                cnt = bank[7][0:NE, 0:P]
                nc.vector.tensor_copy(many[:, 0:NE], bank[7][:, 384:384 + NE])
                nc.vector.memset(small[:, 188 + NE:188 + NEP], 0.0)
                nc.vector.tensor_scalar(novT[0:NE, :], cnt, float(CAP), None, ALU.is_gt)
                for n in range(2 * CAP, S, CAP):
                    dve.drain()
                    nc.vector.tensor_scalar(big[0:NE, 0:P], cnt, float(n), None, ALU.is_gt)
                    dve.drain()
                    nc.vector.tensor_tensor(novT[0:NE, :], novT[0:NE, :], big[0:NE, 0:P], ALU.add)
                dve.drain()
                dve.sem_inc(M["lists"], 1)
                take_list(dve, 0, 0, bank[4])
                one_hot(1)
                take_list(dve, 1, 1, bank[4])
                dve.wait_ge(M["lists"], 5)
                nc.vector.tensor_copy(ovs, bank[7][:, 128:128 + NE])
                nc.vector.tensor_copy(nov, bank[7][:, 256:256 + NE])
                dve.drain()
                for t in range(NT):
                    dve.wait_ge(M["silu"], t + 1)
                    nc.vector.tensor_tensor(shid[:, t, 0:EH], shid[:, t, 256:512], bank[t][:, EH:2 * EH], ALU.mult).then_inc(M["hid"], 1)
                nc.vector.tensor_tensor(oven, ovs, nov, ALU.add)
                dve.drain()
                nc.vector.tensor_copy(ntot, oven[:, NE - 1:NE])
                nc.vector.tensor_tensor(jcmp, oven.unsqueeze(1).to_broadcast([P, NOV, NE]),
                                        C["tile"].unsqueeze(2).to_broadcast([P, NOV, NE]), ALU.is_le)
                dve.drain()
                nc.vector.tensor_reduce(rank2, jcmp, axis=AX_X, op=ALU.add)
                dve.drain()
                nc.vector.tensor_scalar(etab, rank2, float(NE - 1), None, ALU.min)
                nc.vector.tensor_tensor(jcmp, jcmp, nov.unsqueeze(1).to_broadcast([P, NOV, NE]), ALU.mult)
                dve.drain()
                nc.vector.tensor_reduce(rank2, jcmp, axis=AX_X, op=ALU.add)
                dve.drain()
                nc.vector.tensor_tensor(rank2, C["tile"], rank2, ALU.subtract)
                dve.drain()
                nc.vector.tensor_scalar(q128, rank2, 1.0, float(CAP), ALU.add, ALU.mult)
                for t in range(NT):
                    dve.wait_ge(M["dn_done"], t + 1)
                    for i in range(2):
                        hh = h[:, t, i * 512:(i + 1) * 512]
                        nc.vector.tensor_tensor(hh, hh, bank[5 + i if t % 2 == 0 else i][:, :], ALU.add).then_inc(M["dn_out"], 1)

        if "h1" in dbg:
            dump(nc, sem("d4"), dbg["h1"], h[:, :, :])
        if "wts" in dbg:
            dump(nc, sem("d5"), dbg["wts"], tokw[:, 0:NE])
        front.close()
        back = ExitStack()
        ctx.enter_context(back)
        w_hl = back.enter_context(nc.sbuf_tensor("sb_w_hl", [P, 2, 2, 4096], F32R))
        xgT_hl = back.enter_context(nc.sbuf_tensor("sb_xgT_hl", [P, 2, KD, CAP], F32R))
        osb_t = back.enter_context(nc.sbuf_tensor("sb_rows_out", [P, 2, D], F32))
        osb = [osb_t[:, b, :] for b in range(2)]
        wgp = gateT[:, 0:2 * KD, :].rearrange("p (k i) n -> p k (i n)", k=KD)
        s_tail, s_p, s_gp = sem("s_tail"), sem("s_p"), sem("s_gp")
        prow = r1[:, 0:1024].rearrange("p (t n) -> p t n", t=NT)
        wpl = [r1[:, 1024:2048], r1[:, 5120:6144]]
        gple, gfin = r1[:, 2048:3072], r1[:, 3072:4096]

        def load_down(sp, e, b):
            w = a["w_down"][0].rearrange("e (p c) n -> e p c n", c=2)
            sp.dma_start(Wd[b], w[e]).then_inc(s_wd[b], 16)

        def run(eng, step):
            step(0, 0, 0, first=True)
            with eng.Fori(0, NE // 2 - 1) as it:
                step(it * 2 + 1, 1, it)
                step(it * 2 + 2, 0, it + 1)
            step(NE - 1, 1, NE // 2 - 1, final=True)

        def gathered_transposes(pe, half, src, s):
            rows = src.rearrange("q (p k) -> q k p", k=KD)
            for k in range(4 * half, 4 * half + 4):
                last = nc.tensor.transpose(bank[BX[half]][:, (k % 4) * P:(k % 4 + 1) * P], rows[:, k, :], ident)
            last.then_inc(s["xt_pe"], 1)

        def split_up_products(pe, b):
            w = w_hl[:, b].rearrange("p z (i k n) -> p z i k n", i=2, k=KD)
            n = 0
            for k in range(KD):
                for zx, zw in ((0, 0), (0, 1), (1, 0)):
                    last = nc.tensor.matmul(bank[BH][:, :], xgT_hl[:, zx, k, :], w[:, zw, :, k, :], start=n == 0, stop=n == 3 * KD - 1)
                    n += 1
            last.then_inc(E["gu"], 1)

        def hidden_transposes(pe, s):
            rows = hid.rearrange("q (p c) -> q c p", c=2)
            for c in range(2):
                last = nc.tensor.transpose(bank[BT2][:, c * P:(c + 1) * P], rows[:, c, :], ident)
            last.then_inc(s["hT_pe"], 1)

        def down_products(pe, wd, s):
            for i in range(2):
                for c in range(2):
                    last = nc.tensor.matmul(bank[BO[i]][:, :], hT[:, c, :], wd[:, c, i * 512:(i + 1) * 512],
                                            start=c == 0, stop=c == 1)
            last.then_inc(s["dn"], 1)

        with nc.Block() as block:
            @block.sync
            def _(sp):
                def next_gate_up(e, b):
                    for i in range(2):
                        sp.wait_ge(E["lo"], 2 * e + i - 3)
                        sp.sem_inc(s_tick3, 1)
                        load_gu(sp, e, b, i)

                def next_down(e, b):
                    sp.wait_ge(E["dn"], e - 1)
                    sp.sem_inc(s_tick3, 1)
                    load_down(sp, e, b)

                for i in range(2):
                    load_gu(sp, 1, 1, i)
                load_down(sp, 0, 0)
                load_down(sp, 1, 1)
                next_gate_up(2, 0)
                next_gate_up(3, 1)
                with sp.Fori(1, NE // 2 - 1) as it:
                    for b in range(2):
                        next_gate_up(it * 2 + b + 2, b)
                        next_down(it * 2 + b, b)
                next_down(NE - 2, 0)
                sp.wait_ge(E["lo"], 2 * (NE - 1))
                sp.dma_start(prow, a["p"][0, 0].rearrange("(t p) n -> p t n", p=P)).then_inc(s_p, 16)
                sp.dma_start(gple, a["g_ple"][0].partition_broadcast(P)).then_inc(s_gp, 16)
                sp.dma_start(gfin, a["g_final"].partition_broadcast(P)).then_inc(s_gp, 16)
                w_ple = a["w_ple"][0].rearrange("(c p) n -> p c n", p=P)
                sp.dma_start(wpl[0], w_ple[:, 0]).then_inc(s_p, 16)
                next_down(NE - 1, 1)
                sp.wait_ge(E["xt_pe"], 2 * NE)
                sp.dma_start(wpl[1], w_ple[:, 1]).then_inc(s_p, 16)

            @block.gpsimd
            def _(pool):
                def scatter(e, b, it):
                    pool.wait_ge(E["o_dve"], e + 2)
                    pool.wait_ge(E["o_act"], e + 2)
                    pool.sem_inc(s_tick2, 1)
                    by_length(pool, e, lambda n: pool.indirect_dma_start(
                        out=rows_d, out_offset=bass.IndirectOffsetOnAxis(ap=didx[0:n, b:b + 1], axis=0), in_=osb[b][0:n, :],
                        in_offset=None, bounds_check=8 * S - 1, oob_is_err=False).then_inc(stored[b], 16))

                def scattered(b, it):
                    pool.wait_ge(stored[b], 16 * it + 16)
                    pool.sem_inc(row_free, 1)

                pool.sem_inc(row_free, 2)

                def step(e, b, it, first=False, final=False):
                    if not final:
                        pool.wait_ge(E["idx"], e + 3)
                        pool.sem_inc(s_tick2, 1)
                        gather(pool, e + 2, b)
                    if not first:
                        scatter(e - 1, 1 - b, it if b else it - 1)
                        if not final:
                            scattered(1 - b, it if b else it - 1)
                run(pool, step)
                scatter(NE - 1, 1, NE // 2 - 1)
                for b in range(2):
                    scattered(b, NE // 2 - 1)
                pool.wait_ge(xg_f[0], 16 * (NE // 2 + 1))

            @block.tensor
            def _(pe):
                def move_rows(n_gathered, b):
                    pe.wait_ge(xg_f[b], n_gathered)
                    gathered_transposes(pe, 0, xg[b], E)
                    gathered_transposes(pe, 1, xg[b], E)

                def down(e, b, it):
                    pe.wait_ge(E["hT"], e + 1)
                    pe.wait_ge(s_wd[b], 16 * it + 16)
                    pe.wait_ge(E["o_dve"], e + 1)
                    pe.wait_ge(E["o_act"], e + 1)
                    down_products(pe, Wd[b], E)

                move_rows(16, 0)

                def step(e, b, it, first=False, final=False):
                    pe.wait_ge(E["xt_lo"], 2 * e + 2)
                    pe.wait_ge(E["lo"], 2 * e + 2)
                    split_up_products(pe, b)
                    if not final:
                        move_rows(16 * it + 16 + 16 * b, 1 - b)
                        pe.wait_ge(E["oh"], e + 3)
                        list_products(pe, e + 2, E)
                    if not first:
                        down(e - 1, 1 - b, it if b else it - 1)
                    pe.wait_ge(E["hid"], e + 1)
                    hidden_transposes(pe, E)
                run(pe, step)
                down(NE - 1, 1, NE // 2 - 1)

            @block.vector
            def _(dve):
                def rest_of_weights(e, b):
                    for i in range(2):
                        dve.wait_ge(E["hi"], 2 * e + i + 1)
                        cols = slice(2048 * i, 2048 * i + 2048)
                        nc.vector.tensor_tensor(w_hl[:, b, 1, cols], raw[b][:, i, :], w_hl[:, b, 0, cols].bitcast(F32),
                                                ALU.subtract).then_inc(E["lo"], 1)

                def rest_of_rows(e):
                    for half in range(2):
                        dve.wait_ge(E["xt_hi"], 2 * e + half + 1)
                        ks = slice(4 * half, 4 * half + 4)
                        nc.vector.tensor_tensor(xgT_hl[:, 1, ks, :], psv(BX[half], 4, P), xgT_hl[:, 0, ks, :].bitcast(F32),
                                                ALU.subtract).then_inc(E["xt_lo"], 1)

                def rows_out(e, b):
                    dve.wait_ge(E["dn"], e + 1)
                    dve.wait_ge(row_free, e + 1)
                    nc.vector.tensor_copy(didx[:, b:b + 1], dstf[:, bass.ds(e, 1)])
                    nc.vector.tensor_scalar(osb[b][:, 0:512], bank[BO[0]][:, :], wts[:, bass.ds(e, 1)], None, ALU.mult).then_inc(E["o_dve"], 1)

                dve.sem_inc(E["o_dve"], 1)
                rest_of_weights(0, 0)
                rest_of_rows(0)

                def step(e, b, it, first=False, final=False):
                    if not final:
                        one_hot(e + 2)
                        rest_of_weights(e + 1, 1 - b)
                        rest_of_rows(e + 1)
                    dve.wait_ge(E["silu"], e + 1)
                    nc.vector.tensor_tensor(hid, sg, bank[BH][:, EH:2 * EH], ALU.mult).then_inc(E["hid"], 1)
                    if not final:
                        take_list(dve, e + 2, b)
                    if not first:
                        rows_out(e - 1, 1 - b)
                run(dve, step)
                rows_out(NE - 1, 1)

            @block.scalar
            def _(act):
                def round_weights(e, b, it):
                    for i in range(2):
                        act.wait_ge(s_raw[b][i], 16 * it + 16)
                        nc.scalar.copy(w_hl[:, b, 0, 2048 * i:2048 * i + 2048], raw[b][:, i, :]).then_inc(E["hi"], 1)

                def round_rows(e):
                    for half in range(2):
                        act.wait_ge(E["xt_pe"], 2 * e + half + 1)
                        nc.scalar.copy(xgT_hl[:, 0, 4 * half:4 * half + 4, :], psv(BX[half], 4, P)).then_inc(E["xt_hi"], 1)

                def rows_out(e, b):
                    act.wait_ge(E["dn"], e + 1)
                    act.wait_ge(row_free, e + 1)
                    nc.scalar.activation(osb[b][:, 512:1024], bank[BO[1]][:, :], ACT.Copy, scale=wts[:, bass.ds(e, 1)]).then_inc(E["o_act"], 1)

                act.sem_inc(E["o_act"], 1)
                round_weights(0, 0, 0)
                round_rows(0)

                def step(e, b, it, first=False, final=False):
                    if not final:
                        if not first:
                            act.wait_ge(E["gu"], e)
                        round_weights(e + 1, 1 - b, it + 1 if b else it)
                    act.wait_ge(E["gu"], e + 1)
                    nc.scalar.activation(sg, bank[BH][:, 0:EH], ACT.Silu).then_inc(E["silu"], 1)
                    if not final:
                        round_rows(e + 1)
                    if not first:
                        rows_out(e - 1, 1 - b)
                    act.wait_ge(E["hT_pe"], e + 1)
                    nc.scalar.copy(hT, psv(BT2, 2, P)).then_inc(E["hT"], 1)
                run(act, step)
                rows_out(NE - 1, 1)

        V = {n: sem("v_" + n) for n in "oh list idx xg xt_pe xt_dve gate_up gu silu hid hT_pe hT down dn o_act stored".split()}
        slotq, w_v = sg[:, 0:CAP], sg[:, CAP:CAP + 1]
        xgT = osb_t[:, 1, :].rearrange("p (k n) -> p k n", k=KD)
        wgu = raw[1].rearrange("p i (k n) -> p i k n", k=KD)
        with nc.Block() as block:
            @block.sync
            def _(sp):
                more = sp.value_load(ntot[0:1, 0:1], min_val=0, max_val=NOV)
                with sp.If(more > 0):
                    with sp.Fori(0, more) as j:
                        e = sp.value_load(etab[0:1, bass.ds(j, 1)], min_val=0, max_val=NE - 1)
                        for i, n in enumerate(("w_gate", "w_up")):
                            sp.dma_start(raw[1][:, i, :], a[n][0].rearrange("e (p k) n -> e p (k n)", k=KD)[e]).then_inc(V["gate_up"], 16)
                        sp.dma_start(Wd[0], a["w_down"][0].rearrange("e (p c) n -> e p c n", c=2)[e]).then_inc(V["down"], 16)
                        sp.wait_ge(V["stored"], 16 * j + 16)
                        sp.sem_inc(s_tick3, 1)

            @block.gpsimd
            def _(pool):
                more = pool.value_load(ntot[0:1, 0:1], min_val=0, max_val=NOV)
                with pool.If(more > 0):
                    with pool.Fori(0, more) as j:
                        pool.wait_ge(V["idx"], j + 1)
                        pool.sem_inc(s_tick2, 1)
                        pool.indirect_dma_start(out=xg[0], out_offset=None, in_=xn2_d,
                                                in_offset=bass.IndirectOffsetOnAxis(ap=idx[:, 0:1], axis=0),
                                                bounds_check=S - 1, oob_is_err=False).then_inc(V["xg"], 16)
                        pool.wait_ge(V["o_act"], j + 1)
                        pool.sem_inc(s_tick2, 1)
                        pool.indirect_dma_start(out=rows_d, out_offset=bass.IndirectOffsetOnAxis(ap=didx[:, 0:1], axis=0),
                                                in_=osb[0], in_offset=None, bounds_check=8 * S - 1, oob_is_err=False).then_inc(V["stored"], 16)
                        pool.wait_ge(V["stored"], 16 * j + 16)

            @block.tensor
            def _(pe):
                more = pe.value_load(ntot[0:1, 0:1], min_val=0, max_val=NOV)
                with pe.If(more > 0):
                    with pe.Fori(0, more) as j:
                        e = pe.value_load(etab[0:1, bass.ds(j, 1)], min_val=0, max_val=NE - 1)
                        pe.wait_ge(V["oh"], j + 1)
                        list_products(pe, e, V)
                        pe.wait_ge(V["xg"], 16 * j + 16)
                        gathered_transposes(pe, 0, xg[0], V)
                        gathered_transposes(pe, 1, xg[0], V)
                        pe.wait_ge(V["xt_dve"], j + 1)
                        pe.wait_ge(V["gate_up"], 32 * j + 32)
                        for k in range(KD):
                            last = nc.tensor.matmul(bank[BH][:, :], xgT[:, k, :], wgu[:, :, k, :], start=k == 0, stop=k == KD - 1)
                        last.then_inc(V["gu"], 1)
                        pe.wait_ge(V["hid"], j + 1)
                        hidden_transposes(pe, V)
                        pe.wait_ge(V["hT"], j + 1)
                        pe.wait_ge(V["down"], 16 * j + 16)
                        down_products(pe, Wd[0], V)
                        pe.wait_ge(V["o_act"], j + 1)

            @block.vector
            def _(dve):
                more = dve.value_load(ntot[0:1, 0:1], min_val=0, max_val=NOV)
                with dve.If(more > 0):
                    with dve.Fori(0, more) as j:
                        e = dve.value_load(etab[0:1, bass.ds(j, 1)], min_val=0, max_val=NE - 1)
                        nc.vector.tensor_scalar(slotq, C["slot"], q128[:, bass.ds(j, 1)], None, ALU.add)
                        dve.drain()
                        nc.vector.tensor_tensor(onehot, slotq.unsqueeze(1).to_broadcast([P, NT, CAP]),
                                                posm[:, e, :].unsqueeze(2).to_broadcast([P, NT, CAP]), ALU.is_equal).then_inc(V["oh"], 1)
                        dve.wait_ge(V["list"], j + 1)
                        dve.sem_inc(s_tick5, 1)
                        take_numbers(dve, bank[BL], idx[:, 0:1], didx[:, 0:1], w_v, V["idx"])
                        dve.wait_ge(V["xt_pe"], 2 * j + 2)
                        for half in range(2):
                            last = nc.vector.tensor_copy(xgT[:, 4 * half:4 * half + 4, :], psv(BX[half], 4, P))
                        last.then_inc(V["xt_dve"], 1)
                        dve.wait_ge(V["silu"], j + 1)
                        nc.vector.tensor_tensor(hid, hid, bank[BH][:, EH:2 * EH], ALU.mult).then_inc(V["hid"], 1)
                        dve.wait_ge(V["hT_pe"], j + 1)
                        nc.vector.tensor_copy(hT, psv(BT2, 2, P)).then_inc(V["hT"], 1)
                        dve.wait_ge(V["dn"], j + 1)
                        for half in range(2):
                            last = nc.vector.tensor_scalar(osb[0][:, 512 * half:512 * half + 512], bank[BO[half]][:, :], w_v, None, ALU.mult)
                        last.then_inc(V["o_act"], 1)
                        dve.wait_ge(V["stored"], 16 * j + 16)

            @block.scalar
            def _(act):
                more = act.value_load(ntot[0:1, 0:1], min_val=0, max_val=NOV)
                with act.If(more > 0):
                    with act.Fori(0, more) as j:
                        act.wait_ge(V["gu"], j + 1)
                        nc.scalar.activation(hid, bank[BH][:, 0:EH], ACT.Silu).then_inc(V["silu"], 1)
                        act.wait_ge(V["hid"], j + 1)

        back.close()
        xnT = sb("xn3T", [P, KD, 2 * P])
        r2 = sb("rows_even", [P, 8192])
        r3 = sb("rows_odd", [P, 8192])
        pTt = work[:, WORK - D:WORK].rearrange("p (c n) -> p c n", c=2)
        xn3, sigt = sb("xn3", [P, D])[:, :], sb("sig_ple", [P, D])[:, :]
        rows8 = [r2[:, 0:8192].rearrange("p (j n) -> p j n", j=8), r3[:, 0:8192].rearrange("p (j n) -> p j n", j=8)]
        xn3T = xnT[:, :, :].rearrange("p k (b n) -> p b k n", b=2)
        tn = "p_tp p_tc emb_pe emb ms rr xn xt_pe xt gate_pe sig gated ms2 rr2 out".split()
        T = {n: sem("t_" + n) for n in tn}
        s_rows = [[sem(f"t_rows{b}{half}") for half in range(2)] for b in range(2)]
        s_out = sem("s_out")
        part = small[:, 96:112]
        with nc.Block() as block:
            @block.sync
            def _(sp):
                for t in range(NT):
                    if t >= 2:
                        sp.wait_ge(T["ms"], t - 1)
                    for half in range(2):
                        js = slice(4 * half, 4 * half + 4)
                        sp.dma_start(rows8[t % 2][:, js, :], rows_d[t * 8 * P:(t + 1) * 8 * P, :].rearrange("(p j) n -> p j n", j=8)[:, js, :]
                                     ).then_inc(s_rows[t % 2][half], 16)
                    if t == 0:
                        sp.dma_start(wgp, chunks(a["w_ple_gate"][0])).then_inc(s_tail, 16)
                for t in range(NT):
                    sp.wait_ge(T["out"], t + 1)
                    sp.dma_start(a["out"][0, t * P:(t + 1) * P, :], h[:, t, :]).then_inc(s_out, 16)
                sp.wait_ge(s_out, 16 * NT)

            @block.gpsimd
            def _(pool):
                for t in range(NT):
                    for n, (m, r) in enumerate((("ms", "rr"), ("ms2", "rr2"))):
                        if n == 1 and t == 0:
                            continue
                        tt = t - n
                        pool.wait_ge(T[m], tt + 1)
                        nc.gpsimd.tensor_tensor(part[:, 8 * n + 4 + tt:8 * n + 5 + tt], part[:, 8 * n + tt:8 * n + tt + 1],
                                                C["nhalf"][:, 0:1], ALU.pow).then_inc(T[r], 1)
                pool.wait_ge(T["ms2"], NT)
                nc.gpsimd.tensor_tensor(part[:, 15:16], part[:, 11:12], C["nhalf"][:, 0:1], ALU.pow).then_inc(T["rr2"], 1)

            @block.tensor
            def _(pe):
                pe.wait_ge(s_p, 48)
                for c in range(2):
                    for t in range(NT):
                        last = nc.tensor.transpose(bank[c][:, t * P:(t + 1) * P], prow[:, t, c * P:(c + 1) * P], ident)
                    last.then_inc(T["p_tp"], 1)
                pe.wait_ge(T["p_tc"], 2)
                pe.wait_ge(s_p, 48)
                for t in range(NT):
                    if t >= 2:
                        pe.wait_ge(T["emb"], 2 * (t - 1))
                    for i in range(2):
                        for c in range(2):
                            last = nc.tensor.matmul(bank[2 + 2 * (t % 2) + i][:, :], pTt[:, c, t * P:(t + 1) * P],
                                                    wpl[c][:, i * 512:(i + 1) * 512], start=c == 0, stop=c == 1)
                        last.then_inc(T["emb_pe"], 1)
                pe.wait_ge(s_tail, 16)
                for t in range(NT):
                    pe.wait_ge(T["xn"], t + 1)
                    for k in range(KD):
                        last = nc.tensor.transpose(bank[k // 4][:, (k % 4) * P:(k % 4 + 1) * P], xn3[:, k * P:(k + 1) * P], ident)
                    last.then_inc(T["xt_pe"], 1)
                    pe.wait_ge(T["xt"], 2 * t + 2)
                    if t == 0:
                        pe.wait_ge(T["emb"], 8)
                    for i in range(2):
                        for k in range(KD):
                            last = nc.tensor.matmul(bank[2 + 2 * (t % 2) + i][:, :], xn3T[:, t % 2, k, :],
                                                    wgp[:, k, i * 512:(i + 1) * 512], start=k == 0, stop=k == KD - 1)
                        last.then_inc(T["gate_pe"], 1)

            @block.scalar
            def _(act):
                for c in range(2):
                    act.wait_ge(T["p_tp"], c + 1)
                    nc.scalar.copy(pTt[:, c, :], bank[c][:, :]).then_inc(T["p_tc"], 1)
                for t in range(NT):
                    for i in range(2):
                        act.wait_ge(T["emb_pe"], 2 * t + i + 1)
                        nc.scalar.copy(y[:, t, i * 512:(i + 1) * 512], bank[2 + 2 * (t % 2) + i][:, :]).then_inc(T["emb"], 1)
                for t in range(NT):
                    act.wait_ge(T["xt_pe"], t + 1)
                    for i in range(2):
                        nc.scalar.copy(xn3T[:, t % 2, 4 * i:4 * i + 4, :], psv(i, 4, P)).then_inc(T["xt"], 1)
                    if t:
                        act.wait_ge(T["gated"], 2 * t)
                    for i in range(2):
                        act.wait_ge(T["gate_pe"], 2 * t + i + 1)
                        nc.scalar.activation(sigt[:, i * 512:(i + 1) * 512], bank[2 + 2 * (t % 2) + i][:, :], ACT.Sigmoid).then_inc(T["sig"], 1)

            @block.vector
            def _(dve):
                def finish(t):
                    for i in range(2):
                        cols = slice(i * 512, (i + 1) * 512)
                        dve.wait_ge(T["sig"], 2 * t + i + 1)
                        nc.vector.tensor_tensor(y[:, t, cols], y[:, t, cols], sigt[:, cols], ALU.mult).then_inc(T["gated"], 1)
                    dve.drain()
                    nc.vector.tensor_tensor(h[:, t, :], h[:, t, :], y[:, t, :], ALU.add)
                    dve.drain()
                    norm_sums(dve, t, h[:, t, :], y[:, t, :], part[:, 8:12]).then_inc(T["ms2"], 1)
                    dve.wait_ge(T["rr2"], t + 1)
                    nc.vector.scalar_tensor_tensor(out=h[:, t, :], in0=h[:, t, :], scalar=part[:, 12 + t:13 + t], in1=gfin,
                                                   op0=ALU.mult, op1=ALU.mult).then_inc(T["out"], 1)

                dve.wait_ge(s_gp, 32)
                for t in range(NT):
                    r = rows8[t % 2]
                    for half in range(2):
                        dve.wait_ge(s_rows[t % 2][half], 16 * (t // 2) + 16)
                        o = 4 * half
                        nc.vector.tensor_tensor(r[:, o:o + 2, :], r[:, o:o + 2, :], r[:, o + 2:o + 4, :], ALU.add)
                        dve.drain()
                        nc.vector.tensor_tensor(r[:, o, :], r[:, o, :], r[:, o + 1, :], ALU.add)
                        dve.drain()
                        nc.vector.tensor_tensor(h[:, t, :], h[:, t, :], r[:, o, :], ALU.add)
                        if half == 0:
                            dve.drain()
                    dve.drain()
                    norm_sums(dve, t, h[:, t, :], r[:, 1, :], part).then_inc(T["ms"], 1)
                    if t:
                        dve.wait_ge(T["xt_pe"], t)
                    dve.wait_ge(T["rr"], t + 1)
                    nc.vector.scalar_tensor_tensor(out=xn3, in0=h[:, t, :], scalar=part[:, 4 + t:5 + t], in1=gple,
                                                   op0=ALU.mult, op1=ALU.mult).then_inc(T["xn"], 1)
                    if t == 1:
                        dve.wait_ge(T["emb"], 8)
                    if t:
                        finish(t - 1)
                finish(NT - 1)


def dump(nc, s, dst, src):
    with nc.Block() as block:
        @block.sync
        def _(sp):
            sp.dma_start(dst, src).then_inc(s, 16)
            sp.wait_ge(s, 16)


_INS = ["x", "p", "g_mix", "w_in", "cmp_pos_k", "cmp_w1_k", "cmp_b1_k", "cmp_w2_k", "cmp_pos_v", "cmp_w1_v", "cmp_b1_v",
        "cmp_w2_v", "w_branch_a", "w_branch_b", "w_out", "g_ffn", "w_router", "router_bias", "w_gate", "w_up", "w_down",
        "ws_gate", "ws_up", "ws_down", "g_ple", "w_ple_gate", "w_ple", "g_final"]


def kernel(**inputs):
    import concourse.bacc as bacc
    from concourse.bass_utils import run_bass_kernel_spmd

    nc = bacc.Bacc("TRN2", target_bir_lowering=False, num_devices=1)
    arrays = {"in_" + n: np.ascontiguousarray(inputs[n]) for n in _INS}
    arrays["in_cst"] = constants()[0]
    a = {n[3:]: nc.dram_tensor(n, v.shape, mybir.dt.from_np(v.dtype), kind="ExternalInput").ap() for n, v in arrays.items()}
    a["out"] = nc.dram_tensor("out_0", (1, S, D), F32, kind="ExternalOutput").ap()
    build(nc, a)
    r = run_bass_kernel_spmd(nc, [arrays], core_ids=[0])
    return r.results[0]["out_0"]
```
